# Optimizing a Trainium2 kernel written in Bass

```python
import math
import jax, jax.numpy as jnp
from jax import lax
import numpy as np

D_MODEL = 2048
BATCH = 1
SEQ = 256
DEPTH = 1
DEC_BATCH = 8
DEC_SEQ = 4
PAST_LEN = 2048
PAGE_SIZE = 128

M_HEADS = 4
M_DV = D_MODEL // 2 // M_HEADS
M_DK = M_DV // 2
M_QK = M_HEADS * M_DK
M_V = M_HEADS * M_DV
M_CHUNK = 64
CONV_W = 4
A_HEADS = 16
A_KV_HEADS = 2
A_HD = D_MODEL // 2 // A_HEADS
A_Q = A_HEADS * A_HD
A_KV = A_KV_HEADS * A_HD
WINDOW = 128
ATT_BLOCK = WINDOW
N_BUCKETS = 32
MAX_DIST = 128
X_HEADS = 4
X_HD = 128
X_W = X_HEADS * X_HD
N_MEM = 256
D_FF = 4 * D_MODEL
EPS = 1e-6
NEG = -1e30
P_IN = 2 * M_QK + 2 * M_V + 2 * M_HEADS + A_Q + 2 * A_KV

kernel_name = 'hymba_mlstm_swa_sink_memxattn_step'

def rms_norm(x, g):
    xf = x.astype(jnp.float32)
    y = xf * lax.rsqrt(jnp.mean(xf * xf, axis=-1, keepdims=True) + EPS)
    return (y * g.astype(jnp.float32)).astype(x.dtype)

def causal_conv(x, buf, w, b):
    L = x.shape[1]
    xp = jnp.concatenate([buf.astype(x.dtype), x], axis=1)
    y = xp[:, 0:L] * w[0]
    for j in range(1, CONV_W):
        y = y + xp[:, j:j + L] * w[j]
    return jax.nn.silu(y + b), xp[:, xp.shape[1] - (CONV_W - 1):]

def t5_bucket(dist):
    n = jnp.maximum(dist, 0)
    max_exact = N_BUCKETS // 2
    nf = jnp.maximum(n, 1).astype(jnp.float32)
    large = max_exact + (jnp.log(nf / max_exact) / math.log(MAX_DIST / max_exact)
                         * (N_BUCKETS - max_exact)).astype(jnp.int32)
    large = jnp.minimum(large, N_BUCKETS - 1)
    return jnp.where(n < max_exact, n, large)

def mlstm_chunkwise(q, k, v, ig, fg, C0, n0, m0):
    B, L, H, DK = q.shape
    c = M_CHUNK if L % M_CHUNK == 0 else L
    nc = L // c
    k = k * (DK ** -0.5)
    lf = jax.nn.log_sigmoid(fg)

    def chunks(t):
        t = t.reshape((B, nc, c) + t.shape[2:])
        return jnp.swapaxes(jnp.moveaxis(t, 1, 0), 2, 3)

    causal = jnp.tril(jnp.ones((c, c), dtype=bool))

    def step(carry, inp):
        C, n, m = carry
        qc, kc, vc, ic, fc = inp
        b = jnp.cumsum(fc, axis=-1)
        D = jnp.where(causal, b[..., :, None] - b[..., None, :] + ic[..., None, :], -jnp.inf)
        inter = b + m[..., None]
        m_t = jnp.maximum(inter, jnp.max(D, axis=-1))
        w_intra = jnp.exp(D - m_t[..., None])
        w_inter = jnp.exp(inter - m_t)
        s = jnp.einsum('bhtd,bhsd->bhts', qc, kc) * w_intra
        num = (w_inter[..., None] * jnp.einsum('bhtd,bhde->bhte', qc, C)
               + jnp.einsum('bhts,bhse->bhte', s, vc))
        den = w_inter * jnp.einsum('bhtd,bhd->bht', qc, n) + jnp.sum(s, axis=-1)
        h = num / jnp.maximum(jnp.abs(den), jnp.exp(-m_t))[..., None]
        m_new = m_t[..., -1]
        decay = jnp.exp(b[..., -1] + m - m_new)
        w_state = jnp.exp(b[..., -1:] - b + ic - m_new[..., None])
        kw = kc * w_state[..., None]
        C_new = decay[..., None, None] * C + jnp.einsum('bhsd,bhse->bhde', kw, vc)
        n_new = decay[..., None] * n + jnp.sum(kw, axis=2)
        return (C_new, n_new, m_new), h

    (C, n, m), h = lax.scan(step, (C0, n0, m0),
                            (chunks(q), chunks(k), chunks(v), chunks(ig), chunks(lf)))
    h = jnp.moveaxis(jnp.swapaxes(h, 2, 3), 0, 1).reshape(B, L, H, v.shape[-1])
    return h, C, n, m

def banded_attention(q, k, v, dist, valid, sinks, rel_bias):
    B, N, Lq, H, D = q.shape
    KVH = k.shape[3]
    G = H // KVH
    Lk = k.shape[2]
    qg = q.reshape(B, N, Lq, KVH, G, D)
    s = jnp.einsum('bnqhgd,bnkhd->bnhgqk', qg, k.astype(q.dtype)).astype(jnp.float32) * (D ** -0.5)
    bias = rel_bias[t5_bucket(dist)].astype(jnp.float32)
    bias = bias.reshape(N, Lq, Lk, KVH, G).transpose(0, 3, 4, 1, 2)
    s = jnp.where(valid[None, :, None, None], s + bias[None], NEG)
    sink = jnp.broadcast_to(sinks.astype(jnp.float32).reshape(1, 1, KVH, G, 1, 1),
                            (B, N, KVH, G, Lq, 1))
    p = jax.nn.softmax(jnp.concatenate([s, sink], axis=-1), axis=-1)[..., :Lk]
    o = jnp.einsum('bnhgqk,bnkhd->bnqhgd', p.astype(v.dtype), v)
    return o.reshape(B, N, Lq, H * D)

def swa_prompt(q, k, v, sinks, rel_bias):
    B, L, H, D = q.shape
    nb = L // ATT_BLOCK

    def band(t):
        tp = jnp.pad(t, ((0, 0), (ATT_BLOCK, 0), (0, 0), (0, 0))).reshape(B, nb + 1, ATT_BLOCK, t.shape[2], D)
        return jnp.concatenate([tp[:, :-1], tp[:, 1:]], axis=2)

    a = jnp.arange(ATT_BLOCK)[:, None]
    j = jnp.arange(2 * ATT_BLOCK)[None, :]
    blk = jnp.arange(nb)[:, None, None]
    dist = jnp.broadcast_to(ATT_BLOCK + a - j, (nb, ATT_BLOCK, 2 * ATT_BLOCK))
    valid = (blk * ATT_BLOCK - ATT_BLOCK + j >= 0) & (dist >= 0) & (dist < WINDOW)
    o = banded_attention(q.reshape(B, nb, ATT_BLOCK, H, D), band(k), band(v), dist, valid, sinks, rel_bias)
    return o.reshape(B, L, H * D)

def swa_step(q, k, v, win_k, win_v, sinks, rel_bias):
    B, L, H, D = q.shape
    W = win_k.shape[1]
    kb = jnp.concatenate([win_k.astype(k.dtype), k], axis=1)
    vb = jnp.concatenate([win_v.astype(v.dtype), v], axis=1)
    dist = (W + jnp.arange(L)[:, None] - jnp.arange(W + L)[None, :])[None]
    valid = (dist >= 0) & (dist < WINDOW)
    o = banded_attention(q[:, None], kb[:, None], vb[:, None], dist, valid, sinks, rel_bias)
    return o.reshape(B, L, H * D), kb[:, L:], vb[:, L:]

def memory_kv(mem, norm_mem, wk, wv, k_norm):
    B = mem.shape[0]
    mn = rms_norm(mem, norm_mem)
    k = rms_norm((mn @ wk).reshape(B, N_MEM, X_HEADS, X_HD), k_norm)
    v = (mn @ wv).reshape(B, N_MEM, X_HEADS, X_HD)
    return k, v

def cross_attend(h, mem_k, mem_v, wq, q_norm, wo):
    B, L, _ = h.shape
    q = rms_norm((h @ wq).reshape(B, L, X_HEADS, X_HD), q_norm)
    s = jnp.einsum('blhd,bmhd->bhlm', q, mem_k.astype(q.dtype)).astype(jnp.float32) * (X_HD ** -0.5)
    p = jax.nn.softmax(s, axis=-1).astype(q.dtype)
    o = jnp.einsum('bhlm,bmhd->blhd', p, mem_v.astype(q.dtype)).reshape(B, L, X_W)
    return o @ wo

def trunk_layer(x, conv_buf, C0, n0, m0, win_k, win_v, mem_k, mem_v, rel_bias, p):
    B, L, _ = x.shape
    f32 = jnp.float32
    h = rms_norm(x, p['norm_mix'])
    proj = h @ p['w_in']
    sizes = [2 * M_QK, M_V, M_V, M_HEADS, M_HEADS, A_Q, A_KV, A_KV]
    idx = np.cumsum(sizes)[:-1].tolist()
    qk_m, v_m, o_m, ig, fg, q_a, k_a, v_a = jnp.split(proj, idx, axis=-1)
    qk_m, new_conv = causal_conv(qk_m, conv_buf, p['conv_w'], p['conv_b'])
    q_m, k_m = jnp.split(qk_m, 2, axis=-1)
    h_m, C, n, m = mlstm_chunkwise(
        q_m.reshape(B, L, M_HEADS, M_DK).astype(f32), k_m.reshape(B, L, M_HEADS, M_DK).astype(f32),
        v_m.reshape(B, L, M_HEADS, M_DV).astype(f32),
        (ig + p['b_igate']).astype(f32), (fg + p['b_fgate']).astype(f32),
        C0.astype(f32), n0.astype(f32), m0.astype(f32))
    h_m = rms_norm(h_m, p['m_out_norm'].reshape(M_HEADS, M_DV)).reshape(B, L, M_V).astype(x.dtype)
    h_m = h_m * jax.nn.sigmoid(o_m)
    q_a = rms_norm(q_a.reshape(B, L, A_HEADS, A_HD), p['q_norm_a'])
    k_a = rms_norm(k_a.reshape(B, L, A_KV_HEADS, A_HD), p['k_norm_a'])
    v_a = v_a.reshape(B, L, A_KV_HEADS, A_HD)
    if win_k is None:
        a_out = swa_prompt(q_a, k_a, v_a, p['sinks'], rel_bias)
        keep = max(L - WINDOW, 0)
        new_k, new_v = k_a[:, keep:], v_a[:, keep:]
    else:
        a_out, new_k, new_v = swa_step(q_a, k_a, v_a, win_k, win_v, p['sinks'], rel_bias)
    x = x + jnp.concatenate([h_m, a_out.astype(x.dtype)], axis=-1) @ p['w_out']
    x = x + cross_attend(rms_norm(x, p['norm_x']), mem_k, mem_v, p['wq_x'], p['q_norm_x'], p['wo_x'])
    u = rms_norm(x, p['norm_ffn']) @ p['w_up']
    x = x + jnp.square(jax.nn.relu(u)) @ p['w_down']
    dt = x.dtype
    return x, (new_conv, C.astype(dt), n.astype(dt), m.astype(dt), new_k, new_v)

def setup_inputs(seed: int = 0) -> dict:
    key = jax.random.key(seed)
    ks = list(jax.random.split(key, 40))
    cnt = [0]

    def nrm(shape, scale):
        k = ks[cnt[0]]
        cnt[0] += 1
        return scale * jax.random.normal(k, shape, jnp.float32)

    def gain(shape):
        return 1.0 + nrm(shape, 0.05)

    W_BUF = min(WINDOW, PAST_LEN)
    b_f = jnp.broadcast_to(jnp.linspace(3.0, 6.0, M_HEADS, dtype=jnp.float32), (DEPTH, M_HEADS))
    return {
        'x_prompt': nrm((BATCH, SEQ, D_MODEL), 1.0),
        'x_sample': nrm((DEC_BATCH, DEC_SEQ, D_MODEL), 1.0),
        'mem_prompt': nrm((BATCH, N_MEM, D_MODEL), 1.0),
        'state_conv': nrm((DEPTH, DEC_BATCH, CONV_W - 1, 2 * M_QK), 1.0),
        'state_C': nrm((DEPTH, DEC_BATCH, M_HEADS, M_DK, M_DV), 1.0),
        'state_n': nrm((DEPTH, DEC_BATCH, M_HEADS, M_DK), 1.0),
        'state_m': nrm((DEPTH, DEC_BATCH, M_HEADS), 1.0),
        'cache_swa_k': nrm((DEPTH, DEC_BATCH, W_BUF, A_KV_HEADS, A_HD), 1.0),
        'cache_swa_v': nrm((DEPTH, DEC_BATCH, W_BUF, A_KV_HEADS, A_HD), 1.0),
        'cache_mem_k': nrm((DEPTH, DEC_BATCH, N_MEM, X_HEADS, X_HD), 1.0),
        'cache_mem_v': nrm((DEPTH, DEC_BATCH, N_MEM, X_HEADS, X_HD), 1.0),
        'norm_mix': gain((DEPTH, D_MODEL)),
        'w_in': nrm((DEPTH, D_MODEL, P_IN), D_MODEL ** -0.5),
        'conv_w': nrm((DEPTH, CONV_W, 2 * M_QK), CONV_W ** -0.5),
        'conv_b': nrm((DEPTH, 2 * M_QK), 0.02),
        'b_igate': nrm((DEPTH, M_HEADS), 0.1),
        'b_fgate': b_f + nrm((DEPTH, M_HEADS), 0.1),
        'm_out_norm': gain((DEPTH, M_V)),
        'q_norm_a': gain((DEPTH, A_HD)),
        'k_norm_a': gain((DEPTH, A_HD)),
        'sinks': nrm((DEPTH, A_HEADS), 0.5),
        'w_out': nrm((DEPTH, M_V + A_Q, D_MODEL), (M_V + A_Q) ** -0.5),
        'rel_bias': nrm((N_BUCKETS, A_HEADS), 0.5),
        'norm_x': gain((DEPTH, D_MODEL)),
        'norm_mem': gain((DEPTH, D_MODEL)),
        'wq_x': nrm((DEPTH, D_MODEL, X_W), D_MODEL ** -0.5),
        'wk_x': nrm((DEPTH, D_MODEL, X_W), D_MODEL ** -0.5),
        'wv_x': nrm((DEPTH, D_MODEL, X_W), D_MODEL ** -0.5),
        'q_norm_x': gain((DEPTH, X_HD)),
        'k_norm_x': gain((DEPTH, X_HD)),
        'wo_x': nrm((DEPTH, X_W, D_MODEL), X_W ** -0.5),
        'norm_ffn': gain((DEPTH, D_MODEL)),
        'w_up': nrm((DEPTH, D_MODEL, D_FF), D_MODEL ** -0.5),
        'w_down': nrm((DEPTH, D_FF, D_MODEL), D_FF ** -0.5),
    }

def reference(x_prompt, x_sample, mem_prompt, state_conv, state_C, state_n, state_m,
              cache_swa_k, cache_swa_v, cache_mem_k, cache_mem_v,
              norm_mix, w_in, conv_w, conv_b, b_igate, b_fgate, m_out_norm, q_norm_a, k_norm_a,
              sinks, w_out, rel_bias, norm_x, norm_mem, wq_x, wk_x, wv_x, q_norm_x, k_norm_x,
              wo_x, norm_ffn, w_up, w_down):
    f32 = jnp.float32
    Bp = x_prompt.shape[0]
    yp, ys = x_prompt, x_sample
    pc, pC, pn, pm, pk, pv, pmk, pmv = [], [], [], [], [], [], [], []
    sc, sC, sn, sm, sk, sv = [], [], [], [], [], []
    for l in range(DEPTH):
        p = dict(norm_mix=norm_mix[l], w_in=w_in[l], conv_w=conv_w[l], conv_b=conv_b[l],
                 b_igate=b_igate[l], b_fgate=b_fgate[l], m_out_norm=m_out_norm[l],
                 q_norm_a=q_norm_a[l], k_norm_a=k_norm_a[l], sinks=sinks[l], w_out=w_out[l],
                 norm_x=norm_x[l], wq_x=wq_x[l], q_norm_x=q_norm_x[l], wo_x=wo_x[l],
                 norm_ffn=norm_ffn[l], w_up=w_up[l], w_down=w_down[l])
        mk, mv = memory_kv(mem_prompt, norm_mem[l], wk_x[l], wv_x[l], k_norm_x[l])
        yp, st_p = trunk_layer(
            yp, jnp.zeros((Bp, CONV_W - 1, 2 * M_QK), yp.dtype),
            jnp.zeros((Bp, M_HEADS, M_DK, M_DV), f32), jnp.zeros((Bp, M_HEADS, M_DK), f32),
            jnp.zeros((Bp, M_HEADS), f32), None, None, mk, mv, rel_bias, p)
        ys, st_s = trunk_layer(
            ys, state_conv[l], state_C[l], state_n[l], state_m[l], cache_swa_k[l], cache_swa_v[l],
            cache_mem_k[l], cache_mem_v[l], rel_bias, p)
        pc.append(st_p[0]); pC.append(st_p[1]); pn.append(st_p[2]); pm.append(st_p[3])
        pk.append(st_p[4]); pv.append(st_p[5]); pmk.append(mk); pmv.append(mv)
        sc.append(st_s[0]); sC.append(st_s[1]); sn.append(st_s[2]); sm.append(st_s[3])
        sk.append(st_s[4]); sv.append(st_s[5])
    p_conv = jnp.stack(pc); p_C = jnp.stack(pC); p_n = jnp.stack(pn); p_m = jnp.stack(pm)
    p_swa_k = jnp.stack(pk); p_swa_v = jnp.stack(pv)
    p_mem_k = jnp.stack(pmk); p_mem_v = jnp.stack(pmv)
    s_conv = jnp.stack(sc); s_C = jnp.stack(sC); s_n = jnp.stack(sn); s_m = jnp.stack(sm)
    s_swa_k = jnp.stack(sk); s_swa_v = jnp.stack(sv)
    return (yp, ys, p_conv, p_C, p_n, p_m, p_swa_k, p_swa_v, p_mem_k, p_mem_v,
            s_conv, s_C, s_n, s_m, s_swa_k, s_swa_v)


_drawn_inputs = setup_inputs


def setup_inputs(seed=0):
    import zlib

    import numpy as np

    out = dict(_drawn_inputs(seed))
    spreads = {}
    factors = {'b_igate': 8.0,
     'm_out_norm': 2.963,
     'q_norm_a': 8.0,
     'sinks': 24.298,
     'norm_x': 8.0,
     'q_norm_x': 8.0}
    for name, (base, spread) in spreads.items():
        noise = np.random.default_rng([zlib.crc32(name.encode()), seed]).standard_normal(out[name].shape)
        drawn = base * np.exp(spread * noise) if base else spread * noise
        out[name] = __import__('jax').numpy.asarray(drawn.astype(out[name].dtype))
    for name, factor in factors.items():
        out[name] = (out[name] * factor).astype(out[name].dtype)
    return out
```

```python
import math
from contextlib import ExitStack, contextmanager

import numpy as np

import concourse.bass as bass
from concourse import mybir

F32 = mybir.dt.float32
F32R = mybir.dt.float32r
ALU = mybir.AluOpType
ACT = mybir.ActivationFunctionType
AX = mybir.AxisListType

P = 128
D = 2048
KT = D // P
SEQ, DB, DL = 256, 8, 4
ND = DB * DL
NT = SEQ + ND
NMEM = 256
MH, MDK, MDV = 4, 128, 256
AH, KVH, HD, WIN = 16, 2, 64, 128
XH, XHD = 4, 128
XW = XH * XHD
FF = 4 * D
CONVW, CONVC = 4, 2 * MH * MDK
NB, MAXD = 32, 128
EPS = 1e-6
NEG = -1e30
PIN = 4360
COL_QK, COL_V, COL_O, COL_G, COL_QA, COL_KA = 0, 1024, 2048, 3072, 3080, 4104

CK = 4
CW = 256
RING = 4
GAIN_DMAS = 12
GB = 4
NE = 384
WG = 192
VW = MDV + 1

MEMK, MEMV, KVA, QA, QKM, VM, OM = 0, 2, 4, 5, 9, 13, 17
WOUT, WQ, WO, FFN = 21, 29, 31, 39
CH_WO = WQ * 4 + 8
CH_FFN = CH_WO + 8
TL_WOUT, TL_WQ, TL_WO, TL_FFN = 2 * WOUT, 2 * WQ, 2 * WO, 2 * FFN

C_ID, C_REV, C_ONE, C_BLK, C_MSK, C_WM, C_GS, C_TBL = 0, 128, 256, 384, 512, 928, 936, 944
C_END = C_TBL + NE + 4 * 160 + 64


def t5_buckets(n):
    exact = NB // 2
    nf = np.maximum(n, 1).astype(np.float32)
    big = exact + (np.log(nf / np.float32(exact)) / np.float32(math.log(MAXD / exact))
                   * np.float32(NB - exact)).astype(np.int32)
    return np.where(n < exact, n, np.minimum(big, NB - 1))


def constants():
    c = np.zeros((P, C_END), np.float32)
    i = np.arange(P)
    c[i, C_ID + i] = 1
    c[i, C_REV + P - 1 - i] = 1
    c[:, C_ONE:C_ONE + P] = 1
    c[:, C_BLK:C_BLK + P] = (i[:, None] // HD == i[None] // HD)
    tri = np.where(i[:, None] <= i[None], 0, 1e30)
    c[:, C_MSK:C_MSK + P] = tri
    c[:, C_MSK + 256:C_MSK + 384] = tri
    d = np.arange(ND)
    same = d[:, None] // DL == d[None] // DL
    c[:ND, C_MSK + 384:C_MSK + 416] = np.where(same & (d[:, None] <= d[None]), 0, 1e30)
    c[:ND, C_WM:C_WM + DB] = d[:, None] // DL == np.arange(DB)[None]

    c[i, C_GS + (i // DL) % 8] = 1

    def onehot(dist):
        ok = (dist >= 0) & (dist < WIN)
        row = np.where(ok, t5_buckets(np.clip(dist, 0, WIN - 1)), NB)
        out = np.zeros((NB + 1, dist.size), np.float32)
        out[row, np.arange(dist.size)] = 1
        return out

    c[:NB + 1, C_TBL:C_TBL + NE] = onehot(np.arange(NE) - 127)
    for l in range(DL):
        at = C_TBL + NE + l * 160
        c[:NB + 1, at:at + WIN] = onehot(WIN + l - np.arange(WIN))
        c[:NB + 1, at + WIN:at + 160] = onehot(l - d % DL)
    at = C_TBL + NE + 640
    for half in range(2):
        own = half * 4 + i // 32
        c[:, at + 32 * half:at + 32 * half + 32] = np.where(own[:, None] == d[None] // DL, 0, NEG)
    return c


ARENA = 18500

SIGNALS = """
a_hi a_lo act_once act_step av_mm bscr_out c_upd chunk_split chunk_used cols_in conv_done
conv_sig conv_y conv_y0 cp_dma cp_out cst_in dve_once dve_step expo_ready ffn_hi ffn_lo gains_in h_fin hb_ready hi_done
hsq_ready kd_T kd_act kd_dve km_in kw_ready kwd_ready kwm_ready m_bc m_cp m_cu m_den m_emx m_hi m_kT m_lo m_mb m_n0 m_n1
m_root m_s m_ss mem_T mem_hi mem_in mem_lo memkv_out mix_hi mix_lo n_col o_gate pe_once pm_ready pn_out
pool_step prob prob_T pw_out q_normed q_rt q_sq q_ss rel_in rs_root rstd_new sc_mm sq_step sq_sum ss_all
state_in stored sw_exp sw_max swa_cache swa_new_out tail_dma tile0_done tile_out u_hi u_lo v_T v_out
vm_in w_exp wg_in xT_in x_T x_exp x_hi x_in x_lo x_max x_normed x_prob x_rt x_sq x_ss x_stage xo_hi xo_lo
xo_mm xp_T xp_out xs_mm xscr_out y_T y_act y_dve
"""
SLOT_SIGNALS = dict(raw_ready=4, c_in=3, c_out=3, bt_in=2, kc_in=2, vdec_in=2)

ONCE = dict(
    pe_once=dict(gains_T=1, xss_bc=1, gates_pre=1, gcols_T=1, state_T=1, bias_mm=1, kv_T=1, kv_rev=1,
                 kw_T=1, dsc_mm=1, dprob_T=1, dout_mm=1, km_T=1, tail_T=1, ncol_T=1, xd_mm=2, xdp_T=1,
                 xdv_mm=2, xdo_T=1),
    act_once=dict(gains_col=1, rm_root=1, x_ssq=3, kss_root=1, rstd_root=1, g_ln=1, gate_rows=1, ktok_out=2,
                  krev_out=1, kw_out=1, d_exp=1, dpw_out=1, da_hi=4, km_out=2, tail_out=2, ncol_out=1, xd_exp=1,
                  xdp_out=2, od_act=1),
    dve_once=dict(eps_ready=1, relb_set=1, wg_split=2, diag_ready=3, memk_ready=8, rstd_x=1,
                  rel_ready=8, g_nz=1, g_exps=1, gcols_out=4, state_out=2, bias_out=5, kdup_out=2, vtok_out=2,
                  vrev_out=1, kw_out2=1, qd_ready=4, d_max=1, dprob=1, dpn_out=1, da_lo=4, vm_ones=2, xd_max=1,
                  xd_prob=1, od_dve=1))


def layer_kernel(nc, ins, outs, consts):
    with ExitStack() as ctx:
        def sb(name, shape, dt=F32):
            return ctx.enter_context(nc.sbuf_tensor(name, shape, dt))

        base = {}
        for owner, given in ONCE.items():
            first = 0
            for name, n in given.items():
                base[name] = (owner, first)
                first += n

        before = {name: first for name, (_, first) in base.items()}
        sem = {name: ctx.enter_context(nc.semaphore(name)) for name in SIGNALS.split()}
        for name, slots in SLOT_SIGNALS.items():
            sem[name] = [ctx.enter_context(nc.semaphore(f"{name}{s}")) for s in range(slots)]

        class Counts:

            def __init__(self, e, own):
                self.e, self.own, self.n, self.turns = e, own, {}, []

            def __call__(self, name=None):
                name = name or self.own
                self.n[name] = self.n.get(name, 0) + 1
                v = self.n[name]
                for i, rate in self.turns:
                    v = i * rate[name] + v
                return base[name][1] + v if name in base else v

            @contextmanager
            def loop(self, iters, **rate):
                rate[self.own] = rate.pop("own", 0)
                so_far = dict(self.n)
                with self.e.Fori(0, iters) as i:
                    self.turns.append((i, rate))
                    yield i
                    self.turns.pop()
                for name in self.n:
                    got = self.n[name] - so_far.get(name, 0)
                    assert got == rate.get(name, 0), (name, got, rate)
                    self.n[name] += got * (iters - 1)

        raw = sb("raw", [P, RING, CK, CW])
        whi = sb("whi", [P, RING, CK, CW], F32R)
        wlo = sb("wlo", [P, RING, CK, CW], F32R)
        act_hi = [sb("a_hi", [P, KT, NT], F32R), sb("b_hi", [P, KT, NT], F32R)]
        act_lo = [sb("a_lo", [P, KT, NT], F32R), sb("b_lo", [P, KT, NT], F32R)]
        wg_raw = sb("wg_raw", [P, WG])
        wg_hi = sb("wg_hi", [P, WG], F32R)
        wg_lo = sb("wg_lo", [P, WG], F32R)
        cst = sb("cst", [P, C_TBL])
        ident, rev, ones, blk = (cst[:, c:c + P] for c in (C_ID, C_REV, C_ONE, C_BLK))
        mask, wmask = cst[:, C_MSK:C_MSK + 416], cst[:, C_WM:C_WM + DB]
        gcol = sb("gcol", [P, 115])
        small = sb("small", [P, 224])
        rstd = sb("rstd", [P, NT])
        nacc = sb("nacc", [P, NT])
        nsq = sb("nsq", [P, NT])
        rows = sb("rows", [MH, 608])
        stash = sb("stash", [P, 8, 27])
        arena = sb("arena", [P, ARENA])

        def view(at, *shape, parts=P):
            n = int(np.prod(shape))
            assert at + n <= ARENA
            v = arena[0:parts, at:at + n]
            if len(shape) == 1:
                return v
            names = "abcdef"[:len(shape)]
            return v.rearrange(f"p ({' '.join(names)}) -> p {' '.join(names)}",
                               **{k: size for k, size in zip(names, shape)})

        xtok, memtok = view(0, 3, D), view(6144, 2, D)
        kvm = view(10240, 2, 2, XW)
        sqdump = view(15600, D)
        xstage = view(12288, 4, NT)
        gains = view(13440, P, parts=115)
        tables = view(13568, 1088)
        relb = view(14656, AH, parts=NB + 1)
        biasrow = view(14672, NE, parts=AH)
        kgain = view(15056, XHD)
        diag = view(15184, 3, P)
        relx = view(0, KVH, DL, 4, 8, DL, parts=NB + 1)
        scrow, n0row = view(1024, CONVC, parts=24), view(2048, P, parts=32)
        grow = view(6144, 11, NT, parts=MH)
        qhat = view(0, 8, NT)
        khat, ktok, vtok = view(2304, NT), view(2592, 3, P), view(2976, 3, P)
        krev, vrev, ktokd = view(3360, 2, 256), view(3872, 2, P), view(4128, 2, 2, 2, HD)
        sc, pT, bias_t = view(4640, 768), view(5408, 768), view(6176, 2, 2, 256)
        qsq, qrt = view(4640, 2, NT), view(5408, 2, NT)
        SW = 7648
        tdec, pTw = view(SW, 2, 2, 160), view(SW + 640, 4, P)
        pTn, qd = view(SW + 1152, 4, P, parts=32), view(SW + 1664, DB, 32)
        kcache, kwT, vcache = (view(SW + 4608 + 1024 * i, DB, P) for i in range(3))
        cring, sigo, qk = view(0, 3, 4, VW), view(SW, 8, NT), view(SW + 2304, 8, NT)
        vm = view(SW + 4608, 3, MH, VW)
        stage, sct = view(16600, 2, 316), view(17616, 8, 24)
        yb, mrt = view(17808, 312), view(18120, NT)
        yconv = [yb, view(SW, 312)]
        MT = 3104
        expo, pm, kw = view(MT, 416), view(MT + 416, 416), view(MT + 832, 2, P)
        wbc, qin, qn = view(MT + 1088, ND), view(MT + 1216, ND), view(MT + 1248, ND)
        hb, den, hsq = view(MT + 1280, 2, NT), view(MT + 1856, NT), view(MT + 2144, 2, NT)
        emx, kwm, kwd = view(MT + 2720, NT), view(MT + 3008, DB, P, parts=32), view(MT + 4032, P, parts=32)
        cprm = view(MT + 4160, VW)
        xT = view(0, KT, NT)
        qx, kmT, vmem = view(4608, XH, NT), view(5760, XH, NMEM), view(6784, 2, XW)
        kdT = view(7808, DB, XH, NMEM)
        vdec = view(7808, DB, 2, XW)
        kraw = view(16000, 2, 2, XW)
        pc, pcT = view(16000, 2, NMEM), view(16512, 2, NMEM)
        xsq, xrt = view(17024, 2, NT), view(17600, 2, NT)
        dsc, pdT, od = view(17024, NMEM), view(17600, 2, P + 16), view(16000, 2, XW)
        stail_late, nrow = view(16000, CONVC, parts=27), view(18200, P, parts=36)
        ur, us = view(4608, 2, NT), view(5184, 2, NT)
        ytok = view(4608, 3, D)

        EPSC, SSX, SSM, RM, KSS, SINKB, SINKD = 0, 1, 4, 6, 8, 24, 40
        MX, NM, SD, ES, SM, GC, WS, WM, N0, NC_, BG, M0C, KINV, SPARE = 42, 46, 50, 54, 58, 64, 76, 88, 120, 152, 188, 190, 200, 210

        def sm_(c, n=1, parts=P):
            return small[0:parts, c:c + n]

        G = [ctx.enter_context(nc.psum_tensor(f"g{i}", [P, 512], F32)) for i in range(GB)]
        M = [ctx.enter_context(nc.psum_tensor(f"m{i}", [P, 512], F32)) for i in range(4)]
        x_scr = nc.dram_tensor("x_scratch", (P, KT, NT), F32).ap()
        b_scr = nc.dram_tensor("bias_scratch", (AH, NE), F32).ap()

        def wout_kt(n):
            return (CK * (n % 4) + 8) % KT

        def cols(w, col, row=0):
            return w[0].rearrange("(k p) c -> p k c", p=P)[:, row:row + CK, col:col + CW]

        straight = []
        for w in (ins["wk_x"], ins["wv_x"]):
            straight += [cols(w, g * CW, 4 * c) for g in range(2) for c in range(4)]
        straight += [cols(ins["w_in"], COL_KA, 4 * c) for c in range(4)]
        for first, groups in ((COL_QA, 4), (COL_QK, 4), (COL_V, 4), (COL_O, 4)):
            straight += [cols(ins["w_in"], first + g * CW, 4 * c) for g in range(groups) for c in range(4)]
        assert len(straight) == WOUT * 4

        block = ctx.enter_context(nc.Block())

        @block.sync
        def _(sp):
            def chunk(slot, src, used):
                if used is not None:
                    sp.wait_ge(sem["chunk_split"], used)
                sp.dma_start(raw[:, slot, :, :], src).then_inc(sem["raw_ready"][slot], 16)

            for j in range(2):
                sp.dma_start(memtok[:, j, :], ins["mem_prompt"][0, j * P:(j + 1) * P, :]).then_inc(sem["mem_in"], 16)
            for c, src in enumerate(straight):
                chunk(c % RING, src, c - RING + 1 if c >= RING else None)

            def wsrc(w, row, col):
                return w[0].rearrange("(k p) c -> p k c", p=P)[:, bass.ds(row, CK), bass.ds(col, CW)]

            with sp.Fori(1, 5) as i:
                for n in range(8):
                    src = wsrc(ins["w_out"], wout_kt(n), i * 512 + ((n // 4) * CW - 512))
                    chunk(n % RING, src, i * 8 + (4 * WOUT + n - RING + 1 - 8))
            for n in range(8):
                c = 4 * WQ + n
                chunk(c % RING, cols(ins["wq_x"], (n // 4) * CW, 4 * (n % 4)), c - RING + 1)
            for n in range(8):
                c = CH_WO + n
                chunk(c % RING, cols(ins["wo_x"], n * CW), c - RING + 1)
            with sp.Fori(0, 4) as q:
                with sp.Fori(0, 4) as i:
                    for n in range(8):
                        src = wsrc(ins["w_up"], 4 * (n % 4), sp.snap(q * 2048 + i * 512 + (n // 4) * CW))
                        chunk(n % RING, src, q * 64 + i * 8 + (CH_FFN + n - RING + 1))
                with sp.Fori(0, 4) as i:
                    for n in range(8):
                        src = wsrc(ins["w_down"], sp.snap(q * 16 + 4 * (n % 4)), sp.snap(i * 512 + (n // 4) * CW))
                        chunk(n % RING, src, q * 64 + i * 8 + (CH_FFN + 32 + n - RING + 1))

        def dec_dst(x, kv, par):
            return x[1][par * HD:(par + 1) * HD, 8 + 4 * kv:12 + 4 * kv, SEQ:NT].rearrange(
                "p t (b l) -> p t b l", l=DL)

        def dec_src(kv, par):
            return M[2][kv * HD:(kv + 1) * HD, 0:256].rearrange(
                "p (b t r l) -> p t b r l", b=DB, t=4, r=2)[:, :, :, par, :]

        def dec_conv(y):
            return bass.AP(y.tensor, y.offset + 259, [list(y.ap[0]), [7, DB], [1, DL]])

        def dz_dst(x, half):
            return x[1][:, 0:XH, SEQ + 16 * half:SEQ + 16 * half + 16].rearrange("p h (b l) -> p h b l", l=DL)

        def dz_src(half):
            m = M[half][:, :]
            return bass.AP(m.tensor, m.offset, [list(m.ap[0]), [P + DL, XH], [32, 4], [1, DL]])

        def rowcast(x, n):
            return bass.AP(x.tensor, x.offset, [[0, P], [1, n]])

        def y_piece(o):
            kt4, j = divmod(o, 3)
            n = P if j < 2 else ND
            return ytok[0:n, j, kt4 * 512:(kt4 + 1) * 512], M[o % 4][0:n, :]

        beside = {c: [] for c in range(4 * WOUT)}
        for c in range(KT):
            beside[c].append(("x_prep", c))
        for j in range(3):
            beside[5 + j].append(("x_squares", j))
        beside[12].append(("mem_norm",))
        for c, what in ((16, "norm_x"), (17, "gates_mm"), (18, "gates_rows"), (20, "columns"), (22, "keys_turn"),
                        (23, "keys_rev"), (30, "dec_keys"), (38, "dec_scores"), (39, "dec_probs"),
                        (40, "dec_out")):
            beside[c].append((what,))
        for n, c in enumerate((21, 24, 25, 28, 29, 32, 33, 36, 37)):
            beside[c].append(("q_norm", n))
        for t in range(9):
            if t:
                beside[41 + 3 * t].append(("swa_probs", t - 1))
                beside[42 + 3 * t].append(("swa_out", t - 1))
            if t < 8:
                beside[41 + 3 * t].append(("swa_scores", t))
                beside[41 + 3 * t].append(("swa_norm", t))
        for ct in range(8):
            beside[4 * QKM + 4 + ct % 2 + 4 * (ct // 2)].append(("conv_taps", ct))
            beside[4 * QKM + 6 + 4 * (ct // 2)].append(("conv_gate", ct))
        for g, c in enumerate((58, 61, 64, 68)):
            beside[c] += [("v_turn", 2 * g), ("v_turn", 2 * g + 1)]
        for h in range(MH):
            for c, what in ((68, "m_scores"), (69, "m_out0"), (70, "m_out1"), (71, "m_state")):
                beside[c + 4 * h].append((what, h))
            if h:
                beside[68 + 4 * h].append(("m_norm", h - 1))
                beside[69 + 4 * h].insert(0, ("m_final", h - 1))

        beside_wq = {5: [("ss", 0)], 6: [("ss", 1)]}
        cross = [("ds", 0), ("ss", 2), ("ds", 1), ("ss", 3), ("xs", 0), ("xm", 0), ("dsb", 0), ("xs", 1), ("dsb", 1),
                 ("xp", 0), ("xo", 0), ("xm", 1), ("da",), ("xs", 2), ("xp", 1), ("xo", 1), ("de",), ("xm", 2), ("dt",),
                 ("xs", 3), ("xp", 2), ("xo", 2), ("dv", 0), ("xm", 3), ("xp", 3), ("xo", 3), ("dv", 1), ("dz",)]

        @block.tensor
        def _(pe):
            def mm(out, lhsT, rhs, start=True, stop=True):
                return pe.matmul(out, lhsT, rhs, start=start, stop=stop, skip_group_check=True)

            def turn(out, in_):
                n = in_.shape[0]
                return pe.transpose(out, in_, ident[0:n, 0:n])

            def chunk(c, t, src, first=True, last=True, tokens=False, more_c=0, more_t=0, kt0=0):
                pe.wait_ge(sem["chunk_split"], more_c + (c + 1))
                s = c % RING
                for j in range(2):
                    g = G[(t + j) % GB]
                    if first and t + j >= GB:
                        pe.wait_ge(sem["tile_out"], more_t + (t + j - GB + 1))
                    for k in range(CK):
                        kt = kt0 + k
                        for i, (w, a) in enumerate(((whi, act_hi[src]), (whi, act_lo[src]), (wlo, act_hi[src]))):
                            beg, end = first and k == 0 and i == 0, last and k == CK - 1 and i == 2
                            if tokens:
                                m = mm(g[:, 0:CW], a[:, kt, j * P:(j + 1) * P], w[:, s, k, :], beg, end)
                            else:
                                m = mm(g[:, 0:NT], w[:, s, k, j * P:(j + 1) * P], a[:, kt, :], beg, end)
                    if last and j == 0:
                        m.then_inc(sem["tile0_done"], 1)
                m.then_inc(sem["chunk_used"], 1)

            def x_prep(kt):
                if kt < 4:
                    pe.wait_ge(sem["mem_hi"], 13 + kt)
                    pe.wait_ge(sem["mem_lo"], 13 + kt)
                else:
                    pe.wait_ge(sem["x_hi"], kt - 3)
                    pe.wait_ge(sem["x_lo"], kt - 3)
                if kt == 0:
                    pe.wait_ge(sem["x_in"], 48)
                for j in range(3):
                    n = P if j < 2 else ND
                    m = turn(M[kt % 4][:, j * P:j * P + n], xtok[0:n, j, kt * P:(kt + 1) * P])
                m.then_inc(sem["x_T"], 1)

            def norm_x():
                pe.wait_ge(sem["dve_once"], before["diag_ready"] + 3)
                pe.wait_ge(sem["x_hi"], 16)
                pe.wait_ge(sem["x_lo"], 16)
                for j in range(3):
                    n = P if j < 2 else ND
                    m = mm(M[0][:, j * P:j * P + n], ones[0:n, :], diag[0:n, j, 0:n])
                m.then_inc(sem["pe_once"], 1)

            def gates_mm():
                pe.wait_ge(sem["dve_once"], before["wg_split"] + 2)
                for kt in range(KT):
                    c = slice(MH * kt, MH * kt + P)
                    for i, (a, w) in enumerate(((act_hi, wg_hi), (act_lo, wg_hi), (act_hi, wg_lo))):
                        m = mm(M[1][:, 0:NT], w[:, c], a[0][:, kt, :], kt == 0 and i == 0, kt == KT - 1 and i == 2)
                m.then_inc(sem["pe_once"], 1)

            def columns():
                pe.wait_ge(sem["act_once"], before["gate_rows"] + 1)
                for r, at in ((7, 0), (2, 64)):
                    for j in range(3):
                        n = P if j < 2 else ND
                        m = pe.transpose(M[2][0:n, at + 4 * j:at + 4 * j + 4], grow[:, r, j * P:j * P + n],
                                         ident[0:MH, 0:MH])
                m.then_inc(sem["pe_once"], 1)
                pe.wait_ge(sem["state_in"], 32)
                for ct in range(8):
                    pe.transpose(M[3][:, 24 * ct:24 * ct + 24], scrow[:, ct * P:(ct + 1) * P], ident[0:24, 0:24])
                pe.transpose(M[3][:, 192:224], n0row[:, :], ident[0:32, 0:32]).then_inc(sem["pe_once"], 1)
                pe.wait_ge(sem["dve_once"], before["rel_ready"] + 8)
                pe.wait_ge(sem["dve_once"], before["rstd_x"] + 1)
                for kv in range(KVH):
                    for l in range(DL):
                        mm(M[0][:, kv * 160:(kv + 1) * 160], relx[:, kv, l].rearrange("p a b c -> p (a b c)"),
                           tables[0:NB + 1, NE + 160 * l:NE + 160 * l + 160], l == 0, l == DL - 1)
                mm(M[1][0:AH, 0:NE], relb[:, :], tables[0:NB + 1, 0:NE]).then_inc(sem["pe_once"], 1)

            def q_norm(n):
                pe.wait_ge(sem["q_sq"], n + 1)
                if n == 0:
                    pe.wait_ge(sem["dve_once"], before["bias_out"] + 5)
                elif n >= 2:
                    pe.wait_ge(sem["q_rt"], n - 1)
                mm(M[n % 2][:, 0:NT], blk, qsq[:, n % 2, :]).then_inc(sem["q_ss"], 1)

            def keys_turn():
                pe.wait_ge(sem["tile_out"], 10)
                pe.wait_ge(sem["q_normed"], 1)
                pe.wait_ge(sem["dve_once"], before["gcols_out"] + 4)
                pe.wait_ge(sem["dve_once"], before["state_out"] + 2)
                for src, m_ in ((khat, M[2]), (stage[:, 1, 0:NT], M[3])):
                    for j in range(3):
                        n = P if j < 2 else ND
                        m = pe.transpose(m_[0:n, j * P:(j + 1) * P], src[:, j * P:j * P + n], ident)
                m.then_inc(sem["pe_once"], 1)

            def keys_rev():
                pe.wait_ge(sem["act_once"], before["ktok_out"] + 2)
                pe.wait_ge(sem["dve_once"], before["vtok_out"] + 2)
                pe.wait_ge(sem["dve_once"], before["kdup_out"] + 2)
                for kv in range(KVH):
                    for j in range(2):
                        mm(M[2][:, kv * 256 + j * P:kv * 256 + (j + 1) * P],
                           ktokd[:, 1 - j, kv].rearrange("p a b -> p (a b)"), rev)
                for j in range(2):
                    m = mm(M[3][:, j * P:(j + 1) * P], rev, vtok[:, 1 - j, :])
                m.then_inc(sem["pe_once"], 1)

            def dec_keys():
                pe.wait_ge(sem["swa_cache"], 32)
                pe.wait_ge(sem["act_once"], before["krev_out"] + 1)
                pe.wait_ge(sem["dve_once"], before["vrev_out"] + 1)
                for b in range(DB):
                    m = pe.transpose(M[2 + b // 4][:, (b % 4) * P:(b % 4 + 1) * P], kcache[:, b, :], ident)
                m.then_inc(sem["pe_once"], 1)

            def dec_scores():
                pe.wait_ge(sem["act_once"], before["kw_out"] + 1)
                pe.wait_ge(sem["dve_once"], before["kw_out2"] + 1)
                pe.wait_ge(sem["dve_once"], before["qd_ready"] + 4)
                for half in range(2):
                    for i in range(4):
                        b = 4 * half + i
                        at = half * 160
                        for kv in range(KVH):
                            h = slice(kv * HD, (kv + 1) * HD)
                            bank = M[2 + kv][32 * i:32 * i + 32, :]
                            mm(bank[:, at:at + WIN], qd[h, b, :], kwT[h, b, :])
                            m = mm(bank[:, at + WIN:at + 160], qd[h, b, :], khat[h, SEQ:NT])
                m.then_inc(sem["pe_once"], 1)

            def dec_probs():
                pe.wait_ge(sem["dve_once"], before["dprob"] + 1)
                pe.wait_ge(sem["q_rt"], 9)
                scd = sc[:, 0:640].rearrange("p (a b) -> p a b", a=4)
                for i in range(4):
                    pe.transpose(M[0][:, i * P:(i + 1) * P], scd[:, i, 0:WIN], ident)
                    m = pe.transpose(M[1][0:32, i * P:(i + 1) * P], scd[:, i, WIN:160], ident)
                m.then_inc(sem["pe_once"], 1)

            def dec_out():
                pe.wait_ge(sem["act_once"], before["dpw_out"] + 1)
                pe.wait_ge(sem["dve_once"], before["dpn_out"] + 1)
                for half in range(2):
                    for i in range(4):
                        b = 4 * half + i
                        for kv in range(KVH):
                            h = slice(kv * HD, (kv + 1) * HD)
                            o = M[2][h, b * 32:(b + 1) * 32]
                            mm(o, vcache[:, b, h], pTw[:, 2 * half + kv, 32 * i:32 * i + 32], True, False)
                            m = mm(o, vtok[0:32, 2, h], pTn[:, 2 * half + kv, 32 * i:32 * i + 32], False, True)
                m.then_inc(sem["pe_once"], 1)

            def swa_scores(t):
                kv = t // 4
                for par in range(2):
                    h = slice(par * HD, (par + 1) * HD)
                    mm(M[par][:, 0:256], qhat[h, t, P:SEQ], krev[h, kv, :])
                    m = mm(M[par][:, 256:384], qhat[h, t, 0:P], krev[h, kv, P:256])
                m.then_inc(sem["sc_mm"], 1)

            def swa_probs(t):
                pe.wait_ge(sem["prob"], t + 1)
                if t == 0:
                    pe.wait_ge(sem["act_once"], before["da_hi"] + 4)
                    pe.wait_ge(sem["dve_once"], before["da_lo"] + 4)
                else:
                    pe.wait_ge(sem["a_hi"], t)
                    pe.wait_ge(sem["a_lo"], t)
                if t >= 5:
                    pe.wait_ge(sem["v_out"], 4 * (t - 4))
                for i in range(4):
                    pe.transpose(M[2][:, i * P:(i + 1) * P], sc[:, i * P:(i + 1) * P], ident)
                for i in range(2):
                    m = pe.transpose(M[3][:, i * P:(i + 1) * P], sc[:, 512 + i * P:512 + (i + 1) * P], ident)
                m.then_inc(sem["prob_T"], 1)

            def swa_out(t):
                pe.wait_ge(sem["pw_out"], t + 1)
                pe.wait_ge(sem["pn_out"], t + 1)
                kv = t // 4
                v = slice(kv * HD, (kv + 1) * HD)
                for par in range(2):
                    h = slice(par * HD, (par + 1) * HD)
                    mm(M[3][h, 384:512], vrev[:, 0, v], pT[:, par * 256:par * 256 + P], True, False)
                    mm(M[3][h, 384:512], vrev[:, 1, v], pT[:, par * 256 + P:par * 256 + 256], False, True)
                    m = mm(M[3][h, 256:384], vrev[:, 1, v], pT[:, 512 + par * P:512 + (par + 1) * P])
                m.then_inc(sem["av_mm"], 1)

            def v_turn(i):
                pe.wait_ge(sem["tile_out"], 2 * VM + i + 1)
                if i % 2 == 0:
                    pe.wait_ge(sem["a_hi"], min(5 + i // 2, 8))
                    pe.wait_ge(sem["a_lo"], min(5 + i // 2, 8))
                for j in range(3):
                    n = P if j < 2 else ND
                    m = pe.transpose(M[2 + i % 2][0:n, j * P:(j + 1) * P], stage[:, i % 2, j * P:j * P + n], ident)
                m.then_inc(sem["v_T"], 1)

            def m_scores(h):
                sel = ident[0:MH, h:h + 1].to_broadcast([MH, P])
                if h == 0:
                    pe.wait_ge(sem["prob"], 8)
                    pe.wait_ge(sem["act_once"], before["gate_rows"] + 1)
                else:
                    pe.wait_ge(sem["c_upd"], 8 * h)
                mm(M[0][:, 0:320], sel, rows[:, 0:320]).then_inc(sem["m_bc"], 1)
                if h == 0:
                    pe.wait_ge(sem["a_hi"], 8)
                    pe.wait_ge(sem["a_lo"], 8)
                pe.wait_ge(sem["conv_done"], 8)
                q, k = qk[:, h, :], qk[:, MH + h, :]
                mm(M[1][:, 0:SEQ], k[:, 0:P], q[:, 0:SEQ])
                mm(M[1][:, SEQ:384], k[:, P:SEQ], q[:, P:SEQ])
                mm(M[1][0:ND, 384:416], k[:, SEQ:NT], q[:, SEQ:NT]).then_inc(sem["m_s"], 1)
                pe.wait_ge(sem["v_out"], 16)
                for j in range(3):
                    n = P if j < 2 else ND
                    m = pe.transpose(M[2][0:n, j * P:(j + 1) * P], k[:, j * P:j * P + n], ident)
                m.then_inc(sem["m_kT"], 1)

            def numer(h, v, bank):
                c = slice(v * P, (v + 1) * P)
                mm(bank[:, 0:SEQ], vm[:, 0, h, c], pm[:, 0:SEQ], True, False)
                mm(bank[:, P:SEQ], vm[:, 1, h, c], pm[:, SEQ:384], False, False)
                mm(bank[:, SEQ:NT], vm[0:ND, 2, h, c], pm[0:ND, 384:416], False, False)
                for b in range(DB):
                    u = 2 * h + b // 4
                    if b % 4 == 0:
                        pe.wait_ge(sem["c_in"][u % 3], 16 * (u // 3 + 1))
                    m = mm(bank[:, SEQ + DL * b:SEQ + DL * (b + 1)], cring[:, u % 3, b % 4, c],
                           qin[:, DL * b:DL * (b + 1)], False, b == DB - 1)
                return m

            def m_out0(h):
                if h:
                    pe.wait_ge(sem["m_root"], h)
                pe.wait_ge(sem["kw_ready"], 2 * h + 2)
                pe.wait_ge(sem["dve_once"], before["vm_ones"] + 2)
                mm(M[3][:, 0:VW], kw[:, 0, :], vm[:, 0, h, :], True, False)
                mm(M[3][:, 0:VW], kw[:, 1, :], vm[:, 1, h, :], False, True).then_inc(sem["m_cp"], 1)
                pe.wait_ge(sem["pm_ready"], 2 * h + 2)
                numer(h, 0, M[2]).then_inc(sem["m_n0"], 1)
                mm(M[0][:, 0:SEQ], ones, pm[:, 0:SEQ], True, False)
                mm(M[0][:, P:SEQ], ones, pm[:, SEQ:384], False, False)
                mm(M[0][:, SEQ:NT], ones[0:ND, :], pm[0:ND, 384:416], False, False)
                mm(M[0][:, SEQ:NT], ones, qn, False, True).then_inc(sem["m_den"], 1)
                sel = ident[0:MH, h:h + 1].to_broadcast([MH, P])
                mm(M[1][:, 0:NT], sel, rows[:, 320:608]).then_inc(sem["m_mb"], 1)

            def m_out1(h):
                pe.wait_ge(sem["cp_out"], h + 1)
                numer(h, 1, M[3]).then_inc(sem["m_n1"], 1)

            def m_state(h):
                pe.wait_ge(sem["kwm_ready"], h + 1)
                for b in range(DB):
                    bank = M[(1, 2, 0, 3)[b % 4]]
                    if b >= 4:
                        pe.wait_ge(sem["c_upd"], 8 * h + b - 3)
                    elif b == 0:
                        pe.wait_ge(sem["m_emx"], h + 1)
                    elif b == 1:
                        pe.wait_ge(sem["hb_ready"], 2 * h + 1)
                    elif b == 3:
                        pe.wait_ge(sem["hb_ready"], 2 * h + 2)
                    mm(bank[:, 0:VW], kwm[:, b, :], vm[0:ND, 2, h, :]).then_inc(sem["m_cu"], 1)

            def m_norm(h):
                pe.wait_ge(sem["hsq_ready"], h + 1)
                pe.wait_ge(sem["c_upd"], 8 * h + 8)
                mm(M[3][:, 0:NT], ones, hsq[:, 0, :], True, False)
                mm(M[3][:, 0:NT], ones, hsq[:, 1, :], False, True).then_inc(sem["m_ss"], 1)

            do = dict(x_prep=x_prep, norm_x=norm_x, gates_mm=gates_mm, columns=columns, q_norm=q_norm,
                      keys_turn=keys_turn, keys_rev=keys_rev, dec_keys=dec_keys, dec_scores=dec_scores,
                      dec_probs=dec_probs, dec_out=dec_out, swa_scores=swa_scores, swa_probs=swa_probs,
                      swa_out=swa_out, v_turn=v_turn, m_scores=m_scores, m_out0=m_out0, m_out1=m_out1,
                      m_state=m_state, m_norm=m_norm)

            pe.wait_ge(sem["cst_in"], 16)
            pe.wait_ge(sem["gains_in"], 16 * GAIN_DMAS)
            pe.transpose(M[3][:, 0:115], gains[:, :], ident[0:115, 0:115]).then_inc(sem["pe_once"], 1)
            pe.wait_ge(sem["mem_in"], 32)
            for kt in range(KT):
                if kt == 3:
                    pe.wait_ge(sem["act_once"], before["gains_col"] + 1)
                if kt >= 4:
                    pe.wait_ge(sem["mem_hi"], kt - 3)
                    pe.wait_ge(sem["mem_lo"], kt - 3)
                for j in range(2):
                    m = turn(M[kt % 4][:, j * P:(j + 1) * P], memtok[:, j, kt * P:(kt + 1) * P])
                m.then_inc(sem["mem_T"], 1)
            pe.wait_ge(sem["mem_hi"], 16)
            pe.wait_ge(sem["mem_lo"], 16)
            for c in range(4 * WOUT):
                g = c // 4
                if g == KVA:
                    pe.wait_ge(sem["x_hi"], CK * (c % 4 + 1))
                    pe.wait_ge(sem["x_lo"], CK * (c % 4 + 1))
                chunk(c, 2 * g, 1 if g < KVA else 0, c % 4 == 0, c % 4 == 3, g < KVA, kt0=CK * (c % 4))
                for what in beside[c]:
                    if what[0] in do:
                        do[what[0]](*what[1:])
            m_norm(MH - 1)

            pe.wait_ge(sem["a_hi"], 8)
            pe.wait_ge(sem["a_lo"], 8)
            with pe.Fori(0, 4) as i:
                for n in range(8):
                    if wout_kt(n) < 8:
                        pe.wait_ge(sem["m_hi"], wout_kt(n) + CK)
                        pe.wait_ge(sem["m_lo"], wout_kt(n) + CK)
                    chunk(4 * WOUT + n, TL_WOUT + 2 * (n // 4), 1, n % 4 == 0, n % 4 == 3,
                          more_c=i * 8, more_t=i * 4, kt0=wout_kt(n))
                    if n % 4 == 1:
                        s = n // 4
                        pe.wait_ge(sem["kc_in"][s], i * 16 + 16)
                        pe.wait_ge(sem["m_root"], 4)
                        for h in range(XH):
                            for mt in range(2):
                                m = pe.transpose(M[2 * s + h // 2][:, (h % 2) * 256 + mt * P:(h % 2) * 256 + mt * P + P],
                                                 kraw[:, s, mt, h * P:(h + 1) * P], ident)
                        m.then_inc(sem["kd_T"], 1)

            def rms_total(n):
                pe.wait_ge(sem["sq_sum"], 16 * (n + 1))
                mm(M[0][:, 0:NT], ones, nacc[:, :]).then_inc(sem["ss_all"], 1)

            def ss(h):
                pe.wait_ge(sem["x_sq"], h + 1)
                if h >= 2:
                    pe.wait_ge(sem["x_rt"], h - 1)
                elif h == 1:
                    pe.wait_ge(sem["act_once"], before["ncol_out"] + 1)
                mm(M[h % 2][:, 0:NT], ones, xsq[:, h % 2, :]).then_inc(sem["x_ss"], 1)

            def dec_row(b, h):
                return mm(G[b // 2][32 * h:32 * h + ND, (b % 2) * NMEM:(b % 2 + 1) * NMEM], qx[:, h, SEQ:NT],
                          kdT[:, b, h, :])

            def ds(h):
                if h == 0:
                    pe.wait_ge(sem["tile_out"], TL_WQ + XH)
                pe.wait_ge(sem["x_normed"], h + 1)
                for b in range(DB):
                    dec_row(b, h)

            def dsb(half):
                pe.wait_ge(sem["x_normed"], XH)
                for b in range(4 * half, 4 * half + 4):
                    for h in (2, 3):
                        m = dec_row(b, h)
                m.then_inc(sem["pe_once"], 1)

            def xs(h):
                if h >= 2:
                    pe.wait_ge(sem["x_prob"], 2 * (h - 1))
                else:
                    pe.wait_ge(sem["x_rt"], h + 3)
                pe.wait_ge(sem["x_normed"], h + 1)
                for j in range(2):
                    m = mm(M[h % 2][:, j * NMEM:(j + 1) * NMEM], qx[:, h, j * P:(j + 1) * P], kmT[:, h, :])
                m.then_inc(sem["xs_mm"], 1)

            def xp(h):
                pe.wait_ge(sem["x_prob"], 2 * h + 2)
                if h:
                    pe.wait_ge(sem["xp_out"], h)
                else:
                    pe.wait_ge(sem["act_once"], before["tail_out"] + 2)
                for j in range(2):
                    for mt in range(2):
                        m = pe.transpose(M[2][:, mt * 256 + j * P:mt * 256 + (j + 1) * P],
                                         pc[:, j, mt * P:(mt + 1) * P], ident)
                m.then_inc(sem["xp_T"], 1)

            def xo(h):
                pe.wait_ge(sem["xp_out"], h + 1)
                if h:
                    pe.wait_ge(sem["xo_hi"], h)
                    pe.wait_ge(sem["xo_lo"], h)
                else:
                    pe.wait_ge(sem["vm_in"], 16)
                for mt in range(2):
                    m = mm(M[3][:, 0:SEQ], vmem[:, mt, h * P:(h + 1) * P], pcT[:, mt, :], mt == 0, mt == 1)
                m.then_inc(sem["xo_mm"], 1)

            def dt():
                pe.wait_ge(sem["dve_once"], before["xd_prob"] + 1)
                for mt in range(2):
                    m = pe.transpose(G[2][:, mt * P:(mt + 1) * P], dsc[:, mt * P:(mt + 1) * P], ident)
                m.then_inc(sem["pe_once"], 1)

            def dv(half):
                pe.wait_ge(sem["act_once"], before["xdp_out"] + 2)
                pe.wait_ge(sem["vdec_in"][half], 64)
                for i in range(4):
                    b = 4 * half + i
                    for mt in range(2):
                        m = mm(G[half][32 * i:32 * i + 32, :], pdT[:, mt, 16 * b:16 * b + 32], vdec[:, b, mt, :],
                               mt == 0, mt == 1)
                m.then_inc(sem["pe_once"], 1)

            def dz():
                pe.wait_ge(sem["x_prob"], 2 * XH)
                pe.wait_ge(sem["act_once"], before["od_act"] + 1)
                pe.wait_ge(sem["dve_once"], before["od_dve"] + 1)
                for half in range(2):
                    for h in range(XH):
                        m = pe.transpose(M[half][:, h * P:(h + 1) * P], od[:, half, h * P:(h + 1) * P], ident)
                m.then_inc(sem["pe_once"], 1)

            do_cross = dict(ss=ss, ds=ds, dsb=dsb, xs=xs, xp=xp, xo=xo, dt=dt, dv=dv, dz=dz)
            for n in range(8):
                if n < 4:
                    pe.wait_ge(sem["mix_hi"], 4 * n + 4)
                    pe.wait_ge(sem["mix_lo"], 4 * n + 4)
                chunk(4 * WQ + n, TL_WQ + 2 * (n // 4), 0, n % 4 == 0, n % 4 == 3, kt0=CK * (n % 4))
                if n == 1:
                    rms_total(0)
                if n == 2:
                    pe.wait_ge(sem["kd_act"], 8)
                    pe.wait_ge(sem["kd_dve"], 8)
                    pe.wait_ge(sem["km_in"], 16)
                    for h in range(XH):
                        for mt in range(2):
                            m = pe.transpose(M[2 + h // 2][:, (h % 2) * 256 + mt * P:(h % 2) * 256 + mt * P + P],
                                             kraw[:, 0, mt, h * P:(h + 1) * P], ident)
                    m.then_inc(sem["pe_once"], 1)
                if n == 3:
                    pe.wait_ge(sem["act_once"], before["km_out"] + 2)
                    pe.wait_ge(sem["rs_root"], 1)
                    for ct in range(8):
                        m = pe.transpose(M[2 + ct // 4][0:27, (ct % 4) * P:(ct % 4 + 1) * P], stash[:, ct, :], ident)
                    m.then_inc(sem["pe_once"], 1)
                    pe.transpose(M[1][0:36, 0:P], sm_(NC_, 36), ident).then_inc(sem["pe_once"], 1)
                for what, h in beside_wq.get(n, ()):
                    ss(h)
            for what in cross:
                if what[0] in do_cross:
                    do_cross[what[0]](*what[1:])

            pe.wait_ge(sem["xo_hi"], XH + 2)
            pe.wait_ge(sem["xo_lo"], XH + 2)
            for n in range(8):
                chunk(CH_WO + n, TL_WO + 2 * n, 1, True, True)

            def up(q, i, skip=0, first=False):
                for n in range(8):
                    if first and n < 4:
                        pe.wait_ge(sem["ffn_hi"], 4 * n + 4)
                        pe.wait_ge(sem["ffn_lo"], 4 * n + 4)
                    chunk(CH_FFN + 8 * skip + n, TL_FFN + 4 * skip + 2 * (n // 4), 0, n % 4 == 0, n % 4 == 3,
                          more_c=q * 64 + i * 8, more_t=q * 32 + i * 4, kt0=CK * (n % 4))
                    if first and n == 1:
                        rms_total(1)

            def down(q, i, skip=0):
                for n in range(8):
                    pe.wait_ge(sem["u_lo"], q * 16 + (4 * skip + CK * (n % 4 + 1)))
                    chunk(CH_FFN + 16 * skip + 32 + n, TL_FFN + 8 * skip + 16 + 2 * (n // 4), 1, n % 4 == 0, n % 4 == 3,
                          more_c=q * 64 + i * 8, more_t=q * 32 + i * 4, kt0=CK * (n % 4))

            up(0, 0, first=True)
            with pe.Fori(0, 3) as i:
                up(0, i, skip=1)
            with pe.Fori(0, 4) as i:
                down(0, i)
            with pe.Fori(0, 3) as q:
                with pe.Fori(0, 4) as i:
                    up(q, i, skip=8)
                with pe.Fori(0, 4) as i:
                    down(q, i, skip=4)

            pe.wait_ge(sem["tile_out"], TL_FFN + 128)
            for kt4 in range(4):
                for j in range(3):
                    n = P if j < 2 else ND
                    o = 3 * kt4 + j
                    if o >= 4:
                        pe.wait_ge(sem["y_act"] if o % 2 else sem["y_dve"], (o - 4) // 2 + 1)
                    for k in range(4):
                        m = pe.transpose(M[o % 4][0:n, k * P:(k + 1) * P], xT[:, 4 * kt4 + k, j * P:j * P + n], ident)
                    m.then_inc(sem["y_T"], 1)

        @block.scalar
        def _(act):
            now = Counts(act, "act_step")

            def A(out, in_, func=ACT.Copy, **kw):
                return act.activation(out, in_, func, **kw)

            def root(out, in_, mean):
                n = in_.shape[0]
                return act.activation(out, in_, ACT.Sqrt, bias=small[0:n, EPSC:EPSC + 1], scale=1.0 / mean)

            def table(func):
                A(sm_(SPARE, 1, 1), sm_(EPSC, 1, 1), func).then_inc(sem["act_step"], 1)
                act.wait_ge(sem["act_step"], now())

            def split(c, more=0, more_raw=0):
                s = c % RING
                act.wait_ge(sem["raw_ready"][s], more_raw + 16 * (c // RING + 1))
                if c >= RING:
                    act.wait_ge(sem["chunk_used"], more + (c - RING + 1))
                act.activation(whi[:, s], raw[:, s], ACT.Copy).then_inc(sem["hi_done"], 1)

            def load(dst, src, signal):
                act.dma_start(dst, src, allow_slow_non_contiguous=src.ap[-1][1] <= 8).then_inc(signal, 16)

            load(cst[:, :], consts[:, 0:C_TBL], sem["cst_in"])
            for at, what, n in ((0, "norm_mix", 16), (16, "norm_mem", 16), (32, "norm_x", 16), (48, "norm_ffn", 16),
                                (64, "conv_b", 8), (104, "m_out_norm", 8), (112, "q_norm_x", 1)):
                load(gains[at:at + n, :], ins[what].rearrange("o (a b) -> (o a) b", b=P), sem["gains_in"])
            load(gains[72:104, :], ins["conv_w"].rearrange("o w (a b) -> (o w a) b", b=P), sem["gains_in"])
            for r, what in ((113, "q_norm_a"), (114, "k_norm_a")):
                for half in range(2):
                    load(gains[r:r + 1, half * HD:(half + 1) * HD], ins[what], sem["gains_in"])
            act.wait_ge(sem["mem_in"], 32)
            xs = ins["x_prompt"][0]
            load(xtok[:, 0, :], xs[0:P, :], sem["x_in"])
            load(xtok[:, 1, :], xs[P:SEQ, :], sem["x_in"])
            load(xtok[0:ND, 2, :], ins["x_sample"].rearrange("b l d -> (b l) d"), sem["x_in"])
            for half in range(2):
                load(wg_raw[:, half * 64:half * 64 + 64].rearrange("p (k c) -> p k c", c=MH),
                     ins["w_in"][0].rearrange("(k p) c -> p k c", p=P)[:, :, COL_G + MH * half:COL_G + MH * half + MH],
                     sem["wg_in"])
            load(tables, consts[:, C_TBL:C_END], sem["cols_in"])
            load(kgain, rowcast(ins["k_norm_x"], XHD), sem["cols_in"])
            load(sm_(SINKB, AH), rowcast(ins["sinks"], AH), sem["cols_in"])
            load(sm_(BG, 1, MH), ins["b_igate"].rearrange("o h -> h o"), sem["cols_in"])
            load(sm_(BG + 1, 1, MH), ins["b_fgate"].rearrange("o h -> h o"), sem["cols_in"])
            load(sm_(M0C, DB, MH), ins["state_m"].rearrange("o b h -> h (o b)"), sem["cols_in"])

            act.wait_ge(sem["pe_once"], before["gains_T"] + 1)
            A(gcol[:, :], M[3][:, 0:115]).then_inc(sem["act_once"], 1)
            act.wait_ge(sem["act_once"], now("gains_col"))
            for kt in range(KT):
                act.wait_ge(sem["mem_T"], kt + 1)
                A(act_hi[1][:, kt, 0:SEQ], M[kt % 4][:, 0:SEQ], scale=gcol[:, 16 + kt:17 + kt]).then_inc(sem["mem_hi"],
                  1)
                act.wait_ge(sem["mem_hi"], now("mem_hi"))
            for c in range(RING - 1):
                split(c)
            act.wait_ge(sem["dve_once"], before["eps_ready"] + 1)
            for j in range(2):
                A(sqdump, memtok[:, j, :], ACT.Square, accum_out=sm_(SSM + j)).then_inc(sem["act_step"], 1)
                act.wait_ge(sem["act_step"], now())
            root(sm_(RM, 2), sm_(SSM, 2), D).then_inc(sem["act_once"], 1)
            act.wait_ge(sem["act_once"], now("rm_root"))

            def x_squares(j):
                n = P if j < 2 else ND
                act.wait_ge(sem["x_in"], 48)
                A(sqdump[0:n, :], xtok[0:n, j, :], ACT.Square, accum_out=sm_(SSX + j, 1, n)).then_inc(sem["act_once"], 1)
                act.wait_ge(sem["act_once"], now("x_ssq"))

            def x_prep(kt):
                act.wait_ge(sem["x_T"], kt + 1)
                if kt >= 4:
                    act.wait_ge(sem["xscr_out"], 16 * (kt // 4))
                A(xstage[:, kt % 4, :], M[kt % 4][:, 0:NT]).then_inc(sem["x_stage"], 1)
                act.wait_ge(sem["x_stage"], now("x_stage"))
                A(act_hi[0][:, kt, :], M[kt % 4][:, 0:NT], scale=gcol[:, kt:kt + 1]).then_inc(sem["x_hi"], 1)
                act.wait_ge(sem["x_hi"], now("x_hi"))

            def mem_norm():
                act.wait_ge(sem["tile_out"], 4)
                for j in range(2):
                    for h in range(XH):
                        A(yb[:, 0:P], kvm[:, j, 0, h * P:(h + 1) * P], ACT.Square,
                          accum_out=sm_(KSS + 4 * j + h)).then_inc(sem["act_step"], 1)
                        act.wait_ge(sem["act_step"], now())
                root(sm_(KINV, 8), sm_(KSS, 8), XHD).then_inc(sem["act_once"], 1)
                act.wait_ge(sem["act_once"], now("kss_root"))

            def norm_x():
                act.wait_ge(sem["pe_once"], before["xss_bc"] + 1)
                root(rstd[:, :], M[0][:, 0:NT], D).then_inc(sem["act_once"], 1)
                act.wait_ge(sem["act_once"], now("rstd_root"))

            def gates_rows():
                act.wait_ge(sem["dve_once"], before["g_nz"] + 1)
                A(grow[:, 3, :], grow[:, 2, :], ACT.Exp).then_inc(sem["act_step"], 1)
                act.wait_ge(sem["act_step"], now())
                A(grow[:, 4, :], grow[:, 3, :], ACT.Ln, bias=1.0).then_inc(sem["act_once"], 1)
                act.wait_ge(sem["act_once"], now("g_ln"))
                act.wait_ge(sem["dve_once"], before["g_exps"] + 1)
                A(rows[:, NT:320], rows[:, NT:320], ACT.Exp).then_inc(sem["act_step"], 1)
                act.wait_ge(sem["act_step"], now())
                A(grow[:, 2, :], grow[:, 2, :], ACT.Exp).then_inc(sem["act_once"], 1)
                act.wait_ge(sem["act_once"], now("gate_rows"))

            def q_norm(n):
                src = khat if n == 0 else qhat[:, n - 1, :]
                act.wait_ge(sem["tile_out"], 9 if n == 0 else 10 + n)
                if n >= 2:
                    act.wait_ge(sem["q_ss"], n - 1)
                A(qsq[:, n % 2, :], src, ACT.Square).then_inc(sem["q_sq"], 1)
                act.wait_ge(sem["q_sq"], now("q_sq"))
                act.wait_ge(sem["q_ss"], n + 1)
                if n >= 2:
                    act.wait_ge(sem["q_normed"], n - 1)
                root(qrt[:, n % 2, :], M[n % 2][:, 0:NT], HD).then_inc(sem["q_rt"], 1)
                act.wait_ge(sem["q_rt"], now("q_rt"))

            def keys_turn():
                act.wait_ge(sem["pe_once"], before["kv_T"] + 1)
                A(ktok[:, 0:2, :], M[2][:, 0:256].rearrange("p (a b) -> p a b", a=2)).then_inc(sem["act_once"], 1)
                act.wait_ge(sem["act_once"], now("ktok_out"))
                A(ktok[0:ND, 2, :], M[2][0:ND, 256:384]).then_inc(sem["act_once"], 1)
                act.wait_ge(sem["act_once"], now("ktok_out"))

            def keys_rev():
                act.wait_ge(sem["pe_once"], before["kv_rev"] + 1)
                A(krev, M[2][:, :].rearrange("p (a b) -> p a b", a=2)).then_inc(sem["act_once"], 1)
                act.wait_ge(sem["act_once"], now("krev_out"))

            def dec_keys():
                act.wait_ge(sem["pe_once"], before["kw_T"] + 1)
                A(kwT[:, 0:4, :], M[2][:, :].rearrange("p (a b) -> p a b", a=4)).then_inc(sem["act_once"], 1)
                act.wait_ge(sem["act_once"], now("kw_out"))

            def exps(n, at, width):
                A(sm_(ES, 4), sm_(SD, 4), ACT.Exp).then_inc(sem["act_step"], 1)
                act.wait_ge(sem["act_step"], now())
                for i in range(n):
                    v = sc[:, at(i):at(i) + width(i)]
                    A(v, v, ACT.Exp, bias=sm_(NM + i), accum_out=sm_(SM + i)).then_inc(sem["act_step"], 1)
                    act.wait_ge(sem["act_step"], now())

            def dec_scores():
                act.wait_ge(sem["dve_once"], before["d_max"] + 1)
                exps(4, lambda i: 160 * i, lambda i: 160)
                A(sm_(ES, 4), sm_(ES, 4)).then_inc(sem["act_once"], 1)
                act.wait_ge(sem["act_once"], now("d_exp"))

            def dec_probs():
                act.wait_ge(sem["pe_once"], before["dprob_T"] + 1)
                A(pTw, M[0][:, :].rearrange("p (a b) -> p a b", a=4)).then_inc(sem["act_once"], 1)
                act.wait_ge(sem["act_once"], now("dpw_out"))

            def dec_out():
                act.wait_ge(sem["pe_once"], before["dout_mm"] + 1)
                for kv in range(KVH):
                    for par in range(2):
                        A(dec_dst(act_hi, kv, par), dec_src(kv, par)).then_inc(sem["act_once"], 1)
                        act.wait_ge(sem["act_once"], now("da_hi"))

            def swa_scores(t):
                act.wait_ge(sem["sw_max"], t + 1)
                exps(4, lambda i: 256 * i if i < 2 else 512 + 128 * (i - 2), lambda i: 256 if i < 2 else 128)
                A(sm_(ES, 4), sm_(ES, 4)).then_inc(sem["sw_exp"], 1)
                act.wait_ge(sem["sw_exp"], now("sw_exp"))

            def swa_probs(t):
                act.wait_ge(sem["prob_T"], t + 1)
                if t:
                    act.wait_ge(sem["av_mm"], t)
                A(pT[:, 0:512], M[2][:, :]).then_inc(sem["pw_out"], 1)
                act.wait_ge(sem["pw_out"], now("pw_out"))

            def swa_out(t):
                act.wait_ge(sem["av_mm"], t + 1)
                A(act_hi[1][:, 8 + t, 0:SEQ], M[3][:, 256:512]).then_inc(sem["a_hi"], 1)
                act.wait_ge(sem["a_hi"], now("a_hi"))

            def v_turn(i):
                act.wait_ge(sem["v_T"], i + 1)
                c = slice((i % 2) * P, (i % 2 + 1) * P)
                A(vm[:, 0:2, i // 2, c],
                  M[2 + i % 2][:, 0:256].rearrange("p (a b) -> p a b", a=2)).then_inc(sem["v_out"], 1)
                act.wait_ge(sem["v_out"], now("v_out"))
                A(vm[0:ND, 2, i // 2, c], M[2 + i % 2][0:ND, 256:384]).then_inc(sem["v_out"], 1)
                act.wait_ge(sem["v_out"], now("v_out"))

            def m_scores(h):
                act.wait_ge(sem["expo_ready"], 3 * h + 3)
                A(expo[:, 0:384], expo[:, 0:384], ACT.Exp, scale=-1.0).then_inc(sem["w_exp"], 1)
                act.wait_ge(sem["w_exp"], now("w_exp"))
                A(expo[0:ND, 384:416], expo[0:ND, 384:416], ACT.Exp, scale=-1.0).then_inc(sem["w_exp"], 1)
                act.wait_ge(sem["w_exp"], now("w_exp"))

            def m_out0(h):
                act.wait_ge(sem["m_cp"], h + 1)
                if h:
                    act.wait_ge(sem["cp_dma"], 16 * h)
                    act.wait_ge(sem["h_fin"], 2 * h)
                A(cprm, M[3][:, 0:VW]).then_inc(sem["cp_out"], 1)
                act.wait_ge(sem["cp_out"], now("cp_out"))
                A(sm_(NC_ + h), cprm[:, MDV:VW]).then_inc(sem["act_step"], 1)
                act.wait_ge(sem["act_step"], now())
                act.wait_ge(sem["m_mb"], h + 1)
                A(emx, M[1][:, 0:NT], ACT.Exp, scale=-1.0).then_inc(sem["m_emx"], 1)
                act.wait_ge(sem["m_emx"], now("m_emx"))

            def m_out1(h):
                act.wait_ge(sem["hb_ready"], 2 * h + 2)
                A(hsq, hb, ACT.Square).then_inc(sem["hsq_ready"], 1)
                act.wait_ge(sem["hsq_ready"], now("hsq_ready"))

            def m_norm(h):
                table(ACT.Sqrt)
                act.wait_ge(sem["m_ss"], h + 1)
                root(mrt, M[3][:, 0:NT], MDV).then_inc(sem["m_root"], 1)
                act.wait_ge(sem["m_root"], now("m_root"))
                if h < MH - 1:
                    table(ACT.Exp)

            def m_final(h):
                for v in range(2):
                    act.wait_ge(sem["h_fin"], 2 * h + v + 1)
                    A(act_hi[1][:, 2 * h + v, :], hb[:, v, :]).then_inc(sem["m_hi"], 1)
                    act.wait_ge(sem["m_hi"], now("m_hi"))

            def conv_taps(ct):
                act.wait_ge(sem["tile_out"], 2 * QKM + ct + 1)
                if ct >= 2:
                    act.wait_ge(sem["conv_done"], ct - 1)
                A(yconv[ct % 2], stage[:, ct % 2, 0:312], ACT.Identity, scale=gcol[:, 72 + ct:73 + ct],
                  bias=gcol[:, 64 + ct:65 + ct]).then_inc(sem["conv_y0"], 1)
                act.wait_ge(sem["conv_y0"], now("conv_y0"))

            def conv_gate(ct):
                y = yconv[ct % 2]
                act.wait_ge(sem["conv_y"], 3 * ct + 3)
                A(qk[:, ct, 0:SEQ], y[:, 0:SEQ], ACT.Sigmoid).then_inc(sem["conv_sig"], 1)
                act.wait_ge(sem["conv_sig"], now("conv_sig"))
                A(qk[:, ct, SEQ:NT].rearrange("p (b l) -> p b l", b=DB), dec_conv(y), ACT.Sigmoid).then_inc(
                    sem["conv_sig"], 1)
                act.wait_ge(sem["conv_sig"], now("conv_sig"))
                if ct % 2:
                    table(ACT.Exp)

            do = dict(x_prep=x_prep, mem_norm=mem_norm, norm_x=norm_x, gates_rows=gates_rows, q_norm=q_norm,
                      keys_turn=keys_turn, keys_rev=keys_rev, dec_keys=dec_keys, dec_scores=dec_scores,
                      dec_probs=dec_probs, dec_out=dec_out, swa_scores=swa_scores, conv_gate=conv_gate, conv_taps=conv_taps,
                      x_squares=x_squares, swa_probs=swa_probs,
                      swa_out=swa_out, v_turn=v_turn, m_scores=m_scores, m_out0=m_out0, m_out1=m_out1, m_norm=m_norm,
                      m_final=m_final)

            for c in range(4 * WOUT):
                split(c + RING - 1)
                if c % 4 == 3:
                    for j in range(2):
                        t = 2 * (c // 4) + j
                        if c // 4 >= OM:
                            act.wait_ge(sem["tile_out"], t + 1)
                            i = t - 2 * OM
                            A(sigo[:, i, :], sigo[:, i, :], ACT.Sigmoid).then_inc(sem["o_gate"], 1)
                            act.wait_ge(sem["o_gate"], now("o_gate"))
                            if j == 1 and c < 4 * WOUT - 1:
                                table(ACT.Exp)
                for what in beside[c]:
                    if what[0] in do:
                        do[what[0]](*what[1:])
            m_norm(MH - 1)
            m_final(MH - 1)

            with now.loop(4, mix_hi=4, kd_act=2) as i:
                for n in range(8):
                    split(4 * WOUT + n + RING - 1, i * 8, i * 32)
                    if n % 4 == 1:
                        s = n // 4
                        act.wait_ge(sem["kd_T"], i * 2 + (s + 1))
                        A(kdT[:, bass.ds(i * 2 + s, 1), 0:2, :].rearrange("p a h m -> p (a h) m"),
                          M[2 * s][:, :].rearrange("p (a b) -> p a b", a=2)).then_inc(sem["kd_act"], 1)
                        act.wait_ge(sem["kd_act"], now("kd_act"))
                    if n % 4 == 3:
                        for j in range(2):
                            m = 2 * (n // 4) + j
                            act.wait_ge(sem["tile_out"], i * 4 + (TL_WOUT + m + 1))
                            A(act_hi[0][:, bass.ds(i * 4 + m, 1), :].rearrange("p a b -> p (a b)"),
                              xT[:, bass.ds(i * 4 + m, 1), :].rearrange("p a b -> p (a b)"),
                              scale=gcol[:, bass.ds(i * 4 + (32 + m), 1)]).then_inc(sem["mix_hi"], 1)
                            act.wait_ge(sem["mix_hi"], now("mix_hi"))

            def ss(h):
                act.wait_ge(sem["tile_out"], TL_WQ + h + 1)
                if h >= 2:
                    act.wait_ge(sem["x_ss"], h - 1)
                A(xsq[:, h % 2, :], qx[:, h, :], ACT.Square).then_inc(sem["x_sq"], 1)
                act.wait_ge(sem["x_sq"], now("x_sq"))
                act.wait_ge(sem["x_ss"], h + 1)
                if h >= 2:
                    act.wait_ge(sem["x_normed"], h - 1)
                root(xrt[:, h % 2, :], M[h % 2][:, 0:NT], XHD).then_inc(sem["x_rt"], 1)
                act.wait_ge(sem["x_rt"], now("x_rt"))
                if h == XH - 1:
                    table(ACT.Exp)

            def xm(h):
                if h:
                    act.wait_ge(sem["xp_T"], h)
                else:
                    act.wait_ge(sem["tail_dma"], 64)
                act.wait_ge(sem["x_max"], h + 1)
                for j in range(2):
                    A(pc[:, j, :], M[h % 2][:, j * NMEM:(j + 1) * NMEM], ACT.Exp, bias=sm_(NM + j), scale=XHD ** -0.5,
                      accum_out=sm_(SM + j)).then_inc(sem["x_exp"], 1)
                    act.wait_ge(sem["x_exp"], now("x_exp"))

            def xp(h):
                act.wait_ge(sem["xp_T"], h + 1)
                if h:
                    act.wait_ge(sem["xo_mm"], h)
                A(pcT, M[2][:, :].rearrange("p (a b) -> p a b", a=2)).then_inc(sem["xp_out"], 1)
                act.wait_ge(sem["xp_out"], now("xp_out"))

            def xo(h):
                act.wait_ge(sem["xo_mm"], h + 1)
                A(act_hi[1][:, h, 0:SEQ], M[3][:, 0:SEQ]).then_inc(sem["xo_hi"], 1)
                act.wait_ge(sem["xo_hi"], now("xo_hi"))

            def de():
                act.wait_ge(sem["dve_once"], before["xd_max"] + 1)
                A(dsc, dsc, ACT.Exp, bias=sm_(NM + 3), scale=XHD ** -0.5, accum_out=sm_(SM + 3)).then_inc(
                    sem["act_once"], 1)
                act.wait_ge(sem["act_once"], now("xd_exp"))

            def dt():
                act.wait_ge(sem["pe_once"], before["xdp_T"] + 1)
                for mt in range(2):
                    A(pdT[:, mt, 0:P].rearrange("p (b h l) -> p h b l", b=DB, h=XH),
                      G[2][:, mt * P:(mt + 1) * P].rearrange("p (h b l) -> p h b l", b=DB, h=XH)).then_inc(
                          sem["act_once"], 1)
                    act.wait_ge(sem["act_once"], now("xdp_out"))

            def dz():
                act.wait_ge(sem["pe_once"], before["xdv_mm"] + 1)
                act.wait_ge(sem["xp_T"], XH)
                A(od[:, 0, :], G[0][:, :]).then_inc(sem["act_once"], 1)
                act.wait_ge(sem["act_once"], now("od_act"))
                act.wait_ge(sem["pe_once"], before["xdo_T"] + 1)
                for half in range(2):
                    A(dz_dst(act_hi, half), dz_src(half)).then_inc(sem["xo_hi"], 1)
                    act.wait_ge(sem["xo_hi"], now("xo_hi"))

            do_cross = dict(ss=ss, xm=xm, xp=xp, xo=xo, de=de, dt=dt, dz=dz)

            for n in range(8):
                split(4 * WQ + n + RING - 1)
                if n == 1:
                    act.wait_ge(sem["ss_all"], 1)
                    root(rstd[:, :], M[0][:, 0:NT], D).then_inc(sem["rs_root"], 1)
                    act.wait_ge(sem["rs_root"], now("rs_root"))
                if n == 2:
                    act.wait_ge(sem["pe_once"], before["km_T"] + 1)
                    for a in range(2):
                        A(kmT[:, 2 * a:2 * a + 2, :],
                          M[2 + a][:, :].rearrange("p (a b) -> p a b", a=2)).then_inc(sem["act_once"], 1)
                        act.wait_ge(sem["act_once"], now("km_out"))
                if n == 3:
                    act.wait_ge(sem["pe_once"], before["tail_T"] + 1)
                    for a in range(2):
                        A(stail_late[:, a * 512:(a + 1) * 512], M[2 + a][0:27, :]).then_inc(sem["act_once"], 1)
                        act.wait_ge(sem["act_once"], now("tail_out"))
                    act.wait_ge(sem["pe_once"], before["ncol_T"] + 1)
                    A(nrow, M[1][0:36, 0:P]).then_inc(sem["act_once"], 1)
                    act.wait_ge(sem["act_once"], now("ncol_out"))
                for what, h in beside_wq.get(n, ()):
                    ss(h)
            for what in cross:
                if what[0] in do_cross:
                    do_cross[what[0]](*what[1:])

            for n in range(8):
                split(CH_WO + n + RING - 1)
                for j in range(2):
                    m = 2 * n + j
                    act.wait_ge(sem["tile_out"], TL_WO + m + 1)
                    A(act_hi[0][:, m, :], xT[:, m, :], scale=gcol[:, 48 + m:49 + m]).then_inc(sem["ffn_hi"], 1)
                    act.wait_ge(sem["ffn_hi"], now("ffn_hi"))
            def up(q, i, skip=0, first=False):
                for n in range(8):
                    split(CH_FFN + 8 * skip + n + RING - 1, q * 64 + i * 8, q * 256 + i * 32)
                    if first and n == 1:
                        act.wait_ge(sem["ss_all"], 2)
                        root(rstd[:, :], M[0][:, 0:NT], D).then_inc(sem["rs_root"], 1)
                        act.wait_ge(sem["rs_root"], now("rs_root"))
                    if n % 4 == 3:
                        for j in range(2):
                            m = 2 * (n // 4) + j
                            act.wait_ge(sem["tile_out"], q * 32 + i * 4 + (TL_FFN + 4 * skip + m + 1))
                            at = i * 4 + (4 * (skip % 4) + m)
                            A(act_hi[1][:, bass.ds(at, 1), :].rearrange("p a b -> p (a b)"), ur[:, j, :],
                              ACT.Square).then_inc(sem["u_hi"], 1)
                            act.wait_ge(sem["u_hi"], now("u_hi"))

            def down(q, i, skip=0, last=False):
                for n in range(RING + 1 if last else 8):
                    split(CH_FFN + 16 * skip + 32 + n + RING - 1, q * 64 + i * 8, q * 256 + i * 32)

            up(0, 0, first=True)
            with now.loop(3, u_hi=4) as i:
                up(0, i, skip=1)
            with now.loop(4) as i:
                down(0, i)
            with now.loop(2, u_hi=16) as q:
                with now.loop(4, u_hi=4) as i:
                    up(q, i, skip=8)
                with now.loop(4) as i:
                    down(q, i, skip=4)
            with now.loop(4, u_hi=4) as i:
                up(3, i)
            with now.loop(3) as i:
                down(3, i)
            down(3, 3, last=True)
            for o in range(1, 12, 2):
                act.wait_ge(sem["y_T"], o + 1)
                A(*y_piece(o)).then_inc(sem["y_act"], 1)
                act.wait_ge(sem["y_act"], now("y_act"))

        @block.vector
        def _(dve):
            now = Counts(dve, "dve_step")

            def copy(out, in_):
                return dve.tensor_copy(out, in_)

            def ts(out, in_, a, op0, b=None, op1=None):
                if op1 is None:
                    return dve.tensor_scalar(out, in_, a, None, op0)
                return dve.tensor_scalar(out, in_, a, b, op0, op1)

            def tt(out, a, b, op):
                return dve.tensor_tensor(out, a, b, op)

            def stt(out, a, s, b, op0, op1):
                return dve.scalar_tensor_tensor(out=out, in0=a, scalar=s, in1=b, op0=op0, op1=op1)

            def recip(x):
                return dve.reciprocal(x, x)

            def f32(x):
                return x.bitcast(F32)

            MUL, ADD, SUB, MAX, MIN = ALU.mult, ALU.add, ALU.subtract, ALU.max, ALU.min

            def split(c, more=0):
                s = c % RING
                dve.wait_ge(sem["hi_done"], more + (c + 1))
                dve.tensor_tensor(wlo[:, s], raw[:, s], f32(whi[:, s]), SUB).then_inc(sem["chunk_split"], 1)

            dve.memset(sm_(EPSC), EPS).then_inc(sem["dve_once"], 1)
            dve.wait_ge(sem["dve_once"], now("eps_ready"))
            dve.memset(relb, NEG).then_inc(sem["dve_once"], 1)
            dve.wait_ge(sem["dve_once"], now("relb_set"))
            for kt in range(KT):
                dve.wait_ge(sem["mem_hi"], kt + 1)
                stt(act_lo[1][:, kt, 0:SEQ], M[kt % 4][:, 0:SEQ], gcol[:, 16 + kt:17 + kt],
                    f32(act_hi[1][:, kt, 0:SEQ]), MUL, SUB).then_inc(sem["mem_lo"], 1)
                dve.wait_ge(sem["mem_lo"], now("mem_lo"))
            for c in range(RING - 1):
                split(c)
            dve.wait_ge(sem["act_once"], before["rm_root"] + 1)
            dve.wait_ge(sem["cst_in"], 16)
            recip(sm_(RM, 2)).then_inc(sem["dve_step"], 1)
            dve.wait_ge(sem["dve_step"], now())
            dve.memset(wg_raw[:, P:WG], 0.0).then_inc(sem["dve_step"], 1)
            dve.wait_ge(sem["dve_step"], now())
            dve.wait_ge(sem["wg_in"], 32)
            copy(wg_hi[:, :], wg_raw[:, :]).then_inc(sem["dve_once"], 1)
            dve.wait_ge(sem["dve_once"], now("wg_split"))
            tt(wg_lo[:, :], wg_raw[:, :], f32(wg_hi[:, :]), SUB).then_inc(sem["dve_once"], 1)
            dve.wait_ge(sem["dve_once"], now("wg_split"))
            dve.wait_ge(sem["cols_in"], 96)
            for kv in range(KVH):
                tt(yb[:, 0:8], sm_(SINKB + 8 * kv, 8), cst[:, C_GS:C_GS + 8], MUL).then_inc(sem["dve_step"], 1)
                dve.wait_ge(sem["dve_step"], now())
                dve.tensor_reduce(sm_(SINKD + kv), yb[:, 0:8], AX.X, ADD).then_inc(sem["dve_step"], 1)
                dve.wait_ge(sem["dve_step"], now())

            def x_squares(j):
                n = P if j < 2 else ND
                dve.wait_ge(sem["act_once"], before["x_ssq"] + j + 1)
                ts(diag[0:n, j, 0:n], ident[0:n, 0:n], sm_(SSX + j, 1, n), MUL).then_inc(sem["dve_once"], 1)
                dve.wait_ge(sem["dve_once"], now("diag_ready"))

            def x_prep(kt):
                dve.wait_ge(sem["x_hi"], kt + 1)
                stt(act_lo[0][:, kt, :], M[kt % 4][:, 0:NT], gcol[:, kt:kt + 1], f32(act_hi[0][:, kt, :]), MUL,
                    SUB).then_inc(sem["x_lo"], 1)
                dve.wait_ge(sem["x_lo"], now("x_lo"))

            def mem_norm():
                dve.wait_ge(sem["act_once"], before["kss_root"] + 1)
                recip(sm_(KINV, 8)).then_inc(sem["dve_step"], 1)
                dve.wait_ge(sem["dve_step"], now())
                for j in range(2):
                    for h in range(XH):
                        k = kvm[:, j, 0, h * P:(h + 1) * P]
                        stt(k, k, sm_(KINV + 4 * j + h), kgain, MUL, MUL).then_inc(sem["dve_once"], 1)
                        dve.wait_ge(sem["dve_once"], now("memk_ready"))

            def norm_x():
                dve.wait_ge(sem["act_once"], before["rstd_root"] + 1)
                recip(rstd[:, :]).then_inc(sem["dve_once"], 1)
                dve.wait_ge(sem["dve_once"], now("rstd_x"))
                dve.wait_ge(sem["rel_in"], 16)
                dve.wait_ge(sem["x_T"], 16)
                dve.memset(relx[:, :], 0.0).then_inc(sem["dve_step"], 1)
                dve.wait_ge(sem["dve_step"], now())
                for kv in range(KVH):
                    for l in range(DL):
                        copy(relx[:, kv, l, :, :, l],
                             relb[:, 8 * kv:8 * kv + 8].unsqueeze(1).to_broadcast([NB + 1, 4, 8])).then_inc(sem["dve_once"], 1)
                        dve.wait_ge(sem["dve_once"], now("rel_ready"))

            def gates_rows():
                ig, z, nz, e, ln, lf, b, g, gs, seg, res = (grow[:, r, :] for r in range(11))
                dve.wait_ge(sem["pe_once"], before["gates_pre"] + 1)
                dve.wait_ge(sem["mem_lo"], 16)
                tt(ig, M[1][0:MH, 0:NT], rstd[0:MH, :], MUL).then_inc(sem["dve_step"], 1)
                dve.wait_ge(sem["dve_step"], now())
                ts(ig, ig, sm_(BG, 1, MH), ADD).then_inc(sem["dve_step"], 1)
                dve.wait_ge(sem["dve_step"], now())
                tt(z, M[1][64:64 + MH, 0:NT], rstd[64:64 + MH, :], MUL).then_inc(sem["dve_step"], 1)
                dve.wait_ge(sem["dve_step"], now())
                ts(z, z, sm_(BG + 1, 1, MH), ADD).then_inc(sem["dve_step"], 1)
                dve.wait_ge(sem["dve_step"], now())
                stt(nz, z, -1.0, z, MUL, MIN).then_inc(sem["dve_once"], 1)
                dve.wait_ge(sem["dve_once"], now("g_nz"))

                def firsts(x):
                    return x[:, SEQ:NT].rearrange("p (b l) -> p b l", l=DL)[:, :, 0]

                dve.memset(seg, 1.0).then_inc(sem["dve_step"], 1)
                dve.wait_ge(sem["dve_step"], now())
                dve.memset(firsts(seg), 0.0).then_inc(sem["dve_step"], 1)
                dve.wait_ge(sem["dve_step"], now())
                dve.memset(res, 0.0).then_inc(sem["dve_step"], 1)
                dve.wait_ge(sem["dve_step"], now())
                dve.memset(firsts(res), -3e38).then_inc(sem["dve_step"], 1)
                dve.wait_ge(sem["dve_step"], now())
                dve.wait_ge(sem["act_once"], before["g_ln"] + 1)
                stt(lf, z, 0.0, ln, MIN, SUB).then_inc(sem["dve_step"], 1)
                dve.wait_ge(sem["dve_step"], now())
                dve.tensor_tensor_scan(b, seg, lf, 0.0, MUL, ADD).then_inc(sem["dve_step"], 1)
                dve.wait_ge(sem["dve_step"], now())
                tt(g, ig, b, SUB).then_inc(sem["dve_step"], 1)
                dve.wait_ge(sem["dve_step"], now())
                copy(gs, g).then_inc(sem["dve_step"], 1)
                dve.wait_ge(sem["dve_step"], now())
                tt(firsts(gs), firsts(g), sm_(M0C, DB, MH), MAX).then_inc(sem["dve_step"], 1)
                dve.wait_ge(sem["dve_step"], now())
                dve.tensor_tensor_scan(rows[:, 0:NT], res, gs, 0.0, ADD, MAX).then_inc(sem["dve_step"], 1)
                dve.wait_ge(sem["dve_step"], now())
                tt(rows[:, 320:608], b, rows[:, 0:NT], ADD).then_inc(sem["dve_step"], 1)
                dve.wait_ge(sem["dve_step"], now())
                Md = rows[:, SEQ:NT].rearrange("p (b l) -> p b l", l=DL)
                m0 = sm_(M0C, DB, MH).unsqueeze(2).to_broadcast([MH, DB, DL])
                tt(rows[:, NT:320].rearrange("p (b l) -> p b l", l=DL), m0, Md, SUB).then_inc(sem["dve_step"], 1)
                dve.wait_ge(sem["dve_step"], now())
                ts(nz[:, 0:SEQ], g[:, 0:SEQ], rows[:, SEQ - 1:SEQ], SUB).then_inc(sem["dve_step"], 1)
                dve.wait_ge(sem["dve_step"], now())
                tt(nz[:, SEQ:NT].rearrange("p (b l) -> p b l", l=DL),
                   g[:, SEQ:NT].rearrange("p (b l) -> p b l", l=DL),
                   Md[:, :, DL - 1].unsqueeze(2).to_broadcast([MH, DB, DL]), SUB).then_inc(sem["dve_once"], 1)
                dve.wait_ge(sem["dve_once"], now("g_exps"))

            def columns():
                dve.wait_ge(sem["pe_once"], before["gcols_T"] + 1)
                for col, at in ((GC, 0), (WS, 64)):
                    copy(sm_(col, 8), M[2][:, at:at + 8]).then_inc(sem["dve_once"], 1)
                    dve.wait_ge(sem["dve_once"], now("gcols_out"))
                    copy(sm_(col + 8, 4, ND), M[2][0:ND, at + 8:at + 12]).then_inc(sem["dve_once"], 1)
                    dve.wait_ge(sem["dve_once"], now("gcols_out"))
                for h in range(MH):
                    ts(sm_(WM + DB * h, DB, ND), wmask[0:ND, :], sm_(WS + 8 + h, 1, ND), MUL, MDK ** -0.5,
                       MUL).then_inc(sem["dve_step"], 1)
                    dve.wait_ge(sem["dve_step"], now())
                dve.wait_ge(sem["pe_once"], before["state_T"] + 1)
                copy(sct, M[3][:, 0:192].rearrange("p (a b) -> p a b", a=8)).then_inc(sem["dve_once"], 1)
                dve.wait_ge(sem["dve_once"], now("state_out"))
                copy(sm_(N0, 32), M[3][:, 192:224]).then_inc(sem["dve_once"], 1)
                dve.wait_ge(sem["dve_once"], now("state_out"))
                dve.wait_ge(sem["pe_once"], before["bias_mm"] + 1)
                T = M[0][:, 0:320].rearrange("p (a b) -> p a b", a=2)
                for half in range(2):
                    copy(tdec[:, half, :, 0:WIN], T[:, :, 0:WIN]).then_inc(sem["dve_once"], 1)
                    dve.wait_ge(sem["dve_once"], now("bias_out"))
                    other = tables[:, NE + 640 + 32 * half:NE + 672 + 32 * half]
                    tt(tdec[:, half, :, WIN:160], T[:, :, WIN:160], other.unsqueeze(1).to_broadcast([P, 2, 32]),
                       ADD).then_inc(sem["dve_once"], 1)
                    dve.wait_ge(sem["dve_once"], now("bias_out"))
                copy(biasrow, M[1][0:AH, 0:NE]).then_inc(sem["dve_once"], 1)
                dve.wait_ge(sem["dve_once"], now("bias_out"))

            def q_norm(n):
                x, g = (khat, 114) if n == 0 else (qhat[:, n - 1, :], 113)
                dve.wait_ge(sem["q_rt"], n + 1)
                recip(qrt[:, n % 2, :]).then_inc(sem["dve_step"], 1)
                dve.wait_ge(sem["dve_step"], now())
                stt(x, x, gcol[:, g:g + 1], qrt[:, n % 2, :], MUL, MUL).then_inc(sem["q_normed"], 1)
                dve.wait_ge(sem["q_normed"], now("q_normed"))
                if n == 8:
                    for kv in range(KVH):
                        for par in range(2):
                            o = qd[kv * HD:(kv + 1) * HD].rearrange("p b (t r l) -> p t b r l", t=4, r=2)[:, :, :, par, :]
                            x = qhat[par * HD:(par + 1) * HD, 4 * kv:4 * kv + 4, SEQ:NT]
                            copy(o, x.rearrange("p t (b l) -> p t b l", l=DL)).then_inc(sem["dve_once"], 1)
                            dve.wait_ge(sem["dve_once"], now("qd_ready"))

            def keys_turn():
                dve.wait_ge(sem["act_once"], before["ktok_out"] + 2)
                m = M[2][:, 0:256].rearrange("p (a k d) -> p a k d", a=2, k=2)
                for dup in range(2):
                    copy(ktokd[:, :, :, dup, :], m).then_inc(sem["dve_once"], 1)
                    dve.wait_ge(sem["dve_once"], now("kdup_out"))
                copy(vtok[:, 0:2, :], M[3][:, 0:256].rearrange("p (a b) -> p a b", a=2)).then_inc(sem["dve_once"], 1)
                dve.wait_ge(sem["dve_once"], now("vtok_out"))
                copy(vtok[0:ND, 2, :], M[3][0:ND, 256:384]).then_inc(sem["dve_once"], 1)
                dve.wait_ge(sem["dve_once"], now("vtok_out"))

            def keys_rev():
                dve.wait_ge(sem["pe_once"], before["kv_rev"] + 1)
                copy(vrev, M[3][:, 0:256].rearrange("p (a b) -> p a b", a=2)).then_inc(sem["dve_once"], 1)
                dve.wait_ge(sem["dve_once"], now("vrev_out"))

            def dec_keys():
                dve.wait_ge(sem["pe_once"], before["kw_T"] + 1)
                copy(kwT[:, 4:8, :], M[3][:, :].rearrange("p (a b) -> p a b", a=4)).then_inc(sem["dve_once"], 1)
                dve.wait_ge(sem["dve_once"], now("kw_out2"))

            def softmax_max(sink):
                mx = sm_(MX, 4).rearrange("p (a b) -> p a b", a=2)
                tt(mx, mx, sink, MAX).then_inc(sem["dve_step"], 1)
                dve.wait_ge(sem["dve_step"], now())
                ts(sm_(NM, 4), sm_(MX, 4), -1.0, MUL).then_inc(sem["dve_step"], 1)
                dve.wait_ge(sem["dve_step"], now())
                return tt(sm_(SD, 4).rearrange("p (a b) -> p a b", a=2), sink, mx, SUB)

            def softmax_sum():
                tt(sm_(SM, 4), sm_(SM, 4), sm_(ES, 4), ADD).then_inc(sem["dve_step"], 1)
                dve.wait_ge(sem["dve_step"], now())
                recip(sm_(SM, 4)).then_inc(sem["dve_step"], 1)
                dve.wait_ge(sem["dve_step"], now())

            def dec_scores():
                dve.wait_ge(sem["pe_once"], before["dsc_mm"] + 1)
                dve.wait_ge(sem["q_ss"], 9)
                dve.wait_ge(sem["q_normed"], 9)
                for kv in range(KVH):
                    stt(sc[:, 0:640].rearrange("p (a k b) -> p a k b", a=2, k=2)[:, :, kv, :],
                        M[2 + kv][:, 0:320].rearrange("p (a b) -> p a b", a=2), HD ** -0.5, tdec[:, :, kv, :], MUL,
                        ADD).then_inc(sem["dve_step"], 1)
                    dve.wait_ge(sem["dve_step"], now())
                s4 = sc[:, 0:640].rearrange("p (a b) -> p a b", a=4)
                dve.tensor_reduce(sm_(MX, 4), s4, AX.X, MAX).then_inc(sem["dve_step"], 1)
                dve.wait_ge(sem["dve_step"], now())
                softmax_max(sm_(SINKD, 2).unsqueeze(1).to_broadcast([P, 2, 2])).then_inc(sem["dve_once"], 1)
                dve.wait_ge(sem["dve_once"], now("d_max"))
                dve.wait_ge(sem["act_once"], before["d_exp"] + 1)
                softmax_sum()
                tt(s4, s4, sm_(SM, 4).unsqueeze(2).to_broadcast([P, 4, 160]), MUL).then_inc(sem["dve_once"], 1)
                dve.wait_ge(sem["dve_once"], now("dprob"))

            def dec_probs():
                dve.wait_ge(sem["pe_once"], before["dprob_T"] + 1)
                copy(pTn, M[1][0:32, :].rearrange("p (a b) -> p a b", a=4)).then_inc(sem["dve_once"], 1)
                dve.wait_ge(sem["dve_once"], now("dpn_out"))

            def dec_out():
                dve.wait_ge(sem["act_once"], before["da_hi"] + 4)
                for kv in range(KVH):
                    for par in range(2):
                        tt(dec_dst(act_lo, kv, par), dec_src(kv, par), f32(dec_dst(act_hi, kv, par)),
                           SUB).then_inc(sem["dve_once"], 1)
                        dve.wait_ge(sem["dve_once"], now("da_lo"))

            def swa_scores(t):
                dve.wait_ge(sem["sc_mm"], t + 1)
                dve.wait_ge(sem["bt_in"][t % 2], 16 * (t // 2 + 1))
                if t:
                    dve.wait_ge(sem["prob_T"], t)
                else:
                    dve.wait_ge(sem["pe_once"], before["dprob_T"] + 1)
                bt = bias_t[:, t % 2]
                s1 = sc[:, 0:512].rearrange("p (a b) -> p a b", a=2)
                s0 = sc[:, 512:768].rearrange("p (a b) -> p a b", a=2)
                for par in range(2):
                    stt(s1[:, par, :], M[par][:, 0:256], HD ** -0.5, bt[:, par, :], MUL, ADD).then_inc(sem["dve_step"],
                        1)
                    dve.wait_ge(sem["dve_step"], now())
                    stt(s0[:, par, :], M[par][:, 256:384], HD ** -0.5, bt[:, par, 0:P], MUL,
                        ADD).then_inc(sem["dve_step"], 1)
                    dve.wait_ge(sem["dve_step"], now())
                dve.tensor_reduce(sm_(MX, 2), s1, AX.X, MAX).then_inc(sem["dve_step"], 1)
                dve.wait_ge(sem["dve_step"], now())
                dve.tensor_reduce(sm_(MX + 2, 2), s0, AX.X, MAX).then_inc(sem["dve_step"], 1)
                dve.wait_ge(sem["dve_step"], now())
                softmax_max(sm_(SINKB + 2 * t, 2).unsqueeze(1).to_broadcast([P, 2, 2])).then_inc(sem["sw_max"], 1)
                dve.wait_ge(sem["sw_max"], now("sw_max"))

            def swa_norm(t):
                s1 = sc[:, 0:512].rearrange("p (a b) -> p a b", a=2)
                s0 = sc[:, 512:768].rearrange("p (a b) -> p a b", a=2)
                dve.wait_ge(sem["sw_exp"], t + 1)
                softmax_sum()
                tt(s1, s1, sm_(SM, 2).unsqueeze(2).to_broadcast([P, 2, 256]), MUL).then_inc(sem["dve_step"], 1)
                dve.wait_ge(sem["dve_step"], now())
                tt(s0, s0, sm_(SM + 2, 2).unsqueeze(2).to_broadcast([P, 2, P]), MUL).then_inc(sem["prob"], 1)
                dve.wait_ge(sem["prob"], now("prob"))

            def swa_probs(t):
                dve.wait_ge(sem["prob_T"], t + 1)
                if t:
                    dve.wait_ge(sem["av_mm"], t)
                copy(pT[:, 512:768], M[3][:, 0:256]).then_inc(sem["pn_out"], 1)
                dve.wait_ge(sem["pn_out"], now("pn_out"))

            def swa_out(t):
                dve.wait_ge(sem["a_hi"], t + 1)
                tt(act_lo[1][:, 8 + t, 0:SEQ], M[3][:, 256:512], f32(act_hi[1][:, 8 + t, 0:SEQ]),
                   SUB).then_inc(sem["a_lo"], 1)
                dve.wait_ge(sem["a_lo"], now("a_lo"))
                if t == 3:
                    dve.wait_ge(sem["pe_once"], before["dout_mm"] + 1)
                    dve.memset(vm[:, 0:2, :, MDV], 1.0).then_inc(sem["dve_once"], 1)
                    dve.wait_ge(sem["dve_once"], now("vm_ones"))
                    dve.memset(vm[0:ND, 2, :, MDV], 1.0).then_inc(sem["dve_once"], 1)
                    dve.wait_ge(sem["dve_once"], now("vm_ones"))

            def m_scores(h):
                dve.wait_ge(sem["m_bc"], h + 1)
                copy(wbc, M[0][:, NT:320]).then_inc(sem["dve_step"], 1)
                dve.wait_ge(sem["dve_step"], now())
                for r, s, c0, c1 in ((0, P, 0, 256), (1, P, 128, 256), (2, ND, 256, 288)):
                    at = (0, 256, 384)[r]
                    stt(expo[0:s, at:at + c1 - c0], M[0][0:s, c0:c1], sm_(GC + 4 * r + h, 1, s),
                        mask[0:s, at:at + c1 - c0], SUB, MAX).then_inc(sem["expo_ready"], 1)
                    dve.wait_ge(sem["expo_ready"], now("expo_ready"))
                if h:
                    dve.wait_ge(sem["m_n1"], h)
                    dve.wait_ge(sem["m_cu"], 8 * h)
                    dve.wait_ge(sem["m_den"], h)
                tt(qin, qk[:, h, SEQ:NT], wbc, MUL).then_inc(sem["dve_step"], 1)
                dve.wait_ge(sem["dve_step"], now())
                n0 = sm_(N0, 32).rearrange("p (b h) -> p b h", h=MH)[:, :, h].unsqueeze(2).to_broadcast([P, DB, DL])
                tt(qn.rearrange("p (b l) -> p b l", l=DL), qin.rearrange("p (b l) -> p b l", l=DL), n0,
                   MUL).then_inc(sem["dve_step"], 1)
                dve.wait_ge(sem["dve_step"], now())
                dve.wait_ge(sem["m_kT"], h + 1)
                for r in range(2):
                    ts(kw[:, r, :], M[2][:, r * P:(r + 1) * P], sm_(WS + 4 * r + h), MUL, MDK ** -0.5,
                       MUL).then_inc(sem["kw_ready"], 1)
                    dve.wait_ge(sem["kw_ready"], now("kw_ready"))
                if h:
                    dve.wait_ge(sem["kwm_ready"], h)
                copy(kwd, M[2][0:ND, 256:384]).then_inc(sem["kwd_ready"], 1)
                dve.wait_ge(sem["kwd_ready"], now("kwd_ready"))
                dve.wait_ge(sem["w_exp"], 2 * h + 2)
                dve.wait_ge(sem["m_s"], h + 1)
                stt(pm[:, 0:384], M[1][:, 0:384], MDK ** -0.5, expo[:, 0:384], MUL, MUL).then_inc(sem["pm_ready"], 1)
                dve.wait_ge(sem["pm_ready"], now("pm_ready"))
                stt(pm[0:ND, 384:416], M[1][0:ND, 384:416], MDK ** -0.5, expo[0:ND, 384:416], MUL,
                    MUL).then_inc(sem["pm_ready"], 1)
                dve.wait_ge(sem["pm_ready"], now("pm_ready"))

            def m_out0(h):
                dve.wait_ge(sem["m_den"], h + 1)
                dve.wait_ge(sem["m_emx"], h + 1)
                if h:
                    dve.wait_ge(sem["m_hi"], 2 * h)
                    dve.wait_ge(sem["m_ss"], h)
                tt(den, M[0][:, 0:NT], emx, MAX).then_inc(sem["dve_step"], 1)
                dve.wait_ge(sem["dve_step"], now())
                stt(den, M[0][:, 0:NT], -1.0, den, MUL, MAX).then_inc(sem["dve_step"], 1)
                dve.wait_ge(sem["dve_step"], now())
                recip(den).then_inc(sem["dve_step"], 1)
                dve.wait_ge(sem["dve_step"], now())
                dve.wait_ge(sem["m_n0"], h + 1)
                tt(hb[:, 0, :], M[2][:, 0:NT], den, MUL).then_inc(sem["hb_ready"], 1)
                dve.wait_ge(sem["hb_ready"], now("hb_ready"))

            def m_out1(h):
                dve.wait_ge(sem["m_n1"], h + 1)
                tt(hb[:, 1, :], M[3][:, 0:NT], den, MUL).then_inc(sem["hb_ready"], 1)
                dve.wait_ge(sem["hb_ready"], now("hb_ready"))

            def m_state(h):
                for b in range(DB):
                    u = 2 * h + b // 4
                    s = u % 3
                    by_row = [sm_(c, 32).rearrange("p (b h) -> p b h", h=MH)[:, 4 * (u % 2):4 * (u % 2) + 4, h]
                              for c in (N0, NC_ + 4)]
                    if b % 4 == 0:
                        dve.wait_ge(sem["c_in"][s], 16 * (u // 3 + 1))
                        copy(cring[:, s, :, MDV], by_row[0]).then_inc(sem["dve_step"], 1)
                        dve.wait_ge(sem["dve_step"], now())
                    dve.wait_ge(sem["m_cu"], 8 * h + b + 1)
                    stt(cring[:, s, b % 4, :], cring[:, s, b % 4, :], wbc[:, DL * b + DL - 1:DL * b + DL],
                        M[(1, 2, 0, 3)[b % 4]][:, 0:VW], MUL, ADD).then_inc(sem["c_upd"], 1)
                    dve.wait_ge(sem["c_upd"], now("c_upd"))
                    if b % 4 == 3:
                        copy(by_row[1], cring[:, s, :, MDV]).then_inc(sem["n_col"], 1)
                        dve.wait_ge(sem["n_col"], now("n_col"))

            def m_final(h):
                dve.wait_ge(sem["o_gate"], 2 * h + 2)
                dve.wait_ge(sem["m_root"], h + 1)
                recip(mrt).then_inc(sem["dve_step"], 1)
                dve.wait_ge(sem["dve_step"], now())
                for v in range(2):
                    x = hb[:, v, :]
                    stt(x, x, gcol[:, 104 + 2 * h + v:105 + 2 * h + v], mrt, MUL, MUL).then_inc(sem["dve_step"], 1)
                    dve.wait_ge(sem["dve_step"], now())
                    tt(x, x, sigo[:, 2 * h + v, :], MUL).then_inc(sem["h_fin"], 1)
                    dve.wait_ge(sem["h_fin"], now("h_fin"))
                for v in range(2):
                    dve.wait_ge(sem["m_hi"], 2 * h + v + 1)
                    tt(act_lo[1][:, 2 * h + v, :], hb[:, v, :], f32(act_hi[1][:, 2 * h + v, :]),
                       SUB).then_inc(sem["m_lo"], 1)
                    dve.wait_ge(sem["m_lo"], now("m_lo"))

            def conv_taps(ct):
                st, y = stage[:, ct % 2, :], yconv[ct % 2]
                copy(stash[:, ct, 0:3], st[:, 256:259]).then_inc(sem["dve_step"], 1)
                dve.wait_ge(sem["dve_step"], now())
                copy(stash[:, ct, 3:27].rearrange("p (b w) -> p b w", w=3),
                     st[:, 259:315].rearrange("p (b w) -> p b w", w=7)[:, :, 4:7]).then_inc(sem["dve_step"], 1)
                dve.wait_ge(sem["dve_step"], now())
                dve.wait_ge(sem["conv_y0"], ct + 1)
                for w in range(1, CONVW):
                    stt(y, st[:, w:w + 312], gcol[:, 72 + 8 * w + ct:73 + 8 * w + ct], y, MUL, ADD).then_inc(
                        sem["conv_y"], 1)
                    dve.wait_ge(sem["conv_y"], now("conv_y"))

            def conv_gate(ct):
                y, d = yconv[ct % 2], qk[:, ct, SEQ:NT].rearrange("p (b l) -> p b l", l=DL)
                dve.wait_ge(sem["conv_sig"], 2 * ct + 2)
                tt(qk[:, ct, 0:SEQ], y[:, 0:SEQ], qk[:, ct, 0:SEQ], MUL).then_inc(sem["dve_step"], 1)
                dve.wait_ge(sem["dve_step"], now())
                tt(d, dec_conv(y), d, MUL).then_inc(sem["conv_done"], 1)
                dve.wait_ge(sem["conv_done"], now("conv_done"))

            do = dict(x_prep=x_prep, mem_norm=mem_norm, norm_x=norm_x, gates_rows=gates_rows, columns=columns,
                      q_norm=q_norm, keys_turn=keys_turn, keys_rev=keys_rev, dec_keys=dec_keys,
                      dec_scores=dec_scores, dec_probs=dec_probs, dec_out=dec_out, swa_scores=swa_scores, swa_norm=swa_norm, conv_gate=conv_gate, conv_taps=conv_taps,
                      x_squares=x_squares,
                      swa_probs=swa_probs, swa_out=swa_out, m_scores=m_scores, m_out0=m_out0, m_out1=m_out1,
                      m_state=m_state, m_final=m_final)

            def stage_conv(ct, g):
                st = stage[:, ct % 2, :]
                dec = st[:, 259:315].rearrange("p (b w) -> p b w", w=7)
                if ct >= 2:
                    dve.wait_ge(sem["conv_y0"], ct - 1)
                dve.memset(st[:, 0:3], 0.0).then_inc(sem["dve_step"], 1)
                dve.wait_ge(sem["dve_step"], now())
                copy(dec[:, :, 0:3], sct[:, ct, :].rearrange("p (b w) -> p b w", w=3)).then_inc(sem["dve_step"], 1)
                dve.wait_ge(sem["dve_step"], now())
                tt(st[:, 3:259], g[:, 0:SEQ], rstd[:, 0:SEQ], MUL).then_inc(sem["dve_step"], 1)
                dve.wait_ge(sem["dve_step"], now())
                tt(dec[:, :, 3:7], g[:, SEQ:NT].rearrange("p (b l) -> p b l", l=DL),
                   rstd[:, SEQ:NT].rearrange("p (b l) -> p b l", l=DL), MUL).then_inc(sem["tile_out"], 1)
                dve.wait_ge(sem["tile_out"], now("tile_out"))

            for c in range(4 * WOUT):
                split(c + RING - 1)
                if c % 4 == 3:
                    q = c // 4
                    for j in range(2):
                        if j == 0:
                            dve.wait_ge(sem["tile0_done"], q + 1)
                        else:
                            dve.wait_ge(sem["chunk_used"], c + 1)
                        g, t = G[(2 * q + j) % GB], 2 * q + j
                        if q < KVA:
                            kv, half = q // 2, q % 2
                            ts(kvm[:, j, kv, half * CW:(half + 1) * CW], g[:, 0:CW], sm_(RM + j),
                               MUL).then_inc(sem["tile_out"], 1)
                            dve.wait_ge(sem["tile_out"], now("tile_out"))
                        elif QKM <= q < VM:
                            if t == 2 * QKM:
                                dve.wait_ge(sem["pe_once"], before["kv_T"] + 1)
                            stage_conv(t - 2 * QKM, g)
                        else:
                            if q < QA:
                                out = khat if j == 0 else stage[:, 1, 0:NT]
                            elif q < QKM:
                                out = qhat[:, t - 2 * QA, :]
                            elif q < OM:
                                i = t - 2 * VM
                                if i < 2:
                                    dve.wait_ge(sem["conv_y0"], 7 + i)
                                else:
                                    dve.wait_ge(sem["v_T"], i - 1)
                                out = stage[:, i % 2, 0:NT]
                            else:
                                out = sigo[:, t - 2 * OM, :]
                            tt(out, g[:, 0:NT], rstd[:, :], MUL).then_inc(sem["tile_out"], 1)
                            dve.wait_ge(sem["tile_out"], now("tile_out"))
                for what in beside[c]:
                    if what[0] in do:
                        do[what[0]](*what[1:])
            m_final(MH - 1)

            def add_x(m, t, i=None, reg=0):
                x = xT[:, m, :] if i is None else xT[:, bass.ds(i * 4 + m, 1), :].rearrange("p a b -> p (a b)")
                tt(x, x, G[t % GB][:, 0:NT], ADD).then_inc(sem["tile_out"], 1)
                dve.wait_ge(sem["tile_out"], now("tile_out"))

            with now.loop(4, tile_out=4, mix_lo=4, kd_dve=2) as i:
                for n in range(8):
                    split(4 * WOUT + n + RING - 1, i * 8)
                    if n % 4 == 1:
                        s = n // 4
                        dve.wait_ge(sem["kd_T"], i * 2 + (s + 1))
                        copy(kdT[:, bass.ds(i * 2 + s, 1), 2:4, :].rearrange("p a h m -> p (a h) m"),
                             M[2 * s + 1][:, :].rearrange("p (a b) -> p a b", a=2)).then_inc(sem["kd_dve"], 1)
                        dve.wait_ge(sem["kd_dve"], now("kd_dve"))
                    if n % 4 == 3:
                        g = n // 4
                        dve.wait_ge(sem["xT_in"], 16)
                        for j in range(2):
                            if j == 0:
                                dve.wait_ge(sem["tile0_done"], i * 2 + (WOUT + g + 1))
                            else:
                                dve.wait_ge(sem["chunk_used"], i * 8 + (4 * WOUT + n + 1))
                            add_x(2 * g + j, TL_WOUT + 2 * g + j, i)
                        for j in range(2):
                            m = 2 * g + j
                            at = bass.ds(i * 4 + m, 1)
                            dve.wait_ge(sem["mix_hi"], i * 4 + (m + 1))
                            stt(act_lo[0][:, at, :].rearrange("p a b -> p (a b)"),
                                xT[:, at, :].rearrange("p a b -> p (a b)"), gcol[:, bass.ds(i * 4 + (32 + m), 1)],
                                f32(act_hi[0][:, at, :]).rearrange("p a b -> p (a b)"), MUL, SUB).then_inc(sem["mix_lo"],
                                1)
                            dve.wait_ge(sem["mix_lo"], now("mix_lo"))

            def ss(h):
                dve.wait_ge(sem["x_rt"], h + 1)
                recip(xrt[:, h % 2, :]).then_inc(sem["dve_step"], 1)
                dve.wait_ge(sem["dve_step"], now())
                stt(qx[:, h, :], qx[:, h, :], gcol[:, 112:113], xrt[:, h % 2, :], MUL, MUL).then_inc(sem["x_normed"], 1)
                dve.wait_ge(sem["x_normed"], now("x_normed"))

            def xm(h):
                dve.wait_ge(sem["xs_mm"], h + 1)
                if h:
                    dve.wait_ge(sem["x_exp"], 2 * h)
                dve.tensor_reduce(sm_(MX, 2), M[h % 2][:, :].rearrange("p (a b) -> p a b", a=2), AX.X,
                                  MAX).then_inc(sem["dve_step"], 1)
                dve.wait_ge(sem["dve_step"], now())
                ts(sm_(NM, 2), sm_(MX, 2), -(XHD ** -0.5), MUL).then_inc(sem["x_max"], 1)
                dve.wait_ge(sem["x_max"], now("x_max"))
                dve.wait_ge(sem["x_exp"], 2 * h + 2)
                recip(sm_(SM, 2)).then_inc(sem["dve_step"], 1)
                dve.wait_ge(sem["dve_step"], now())
                for j in range(2):
                    ts(pc[:, j, :], pc[:, j, :], sm_(SM + j), MUL).then_inc(sem["x_prob"], 1)
                    dve.wait_ge(sem["x_prob"], now("x_prob"))

            def xo(h):
                dve.wait_ge(sem["xo_hi"], h + 1)
                tt(act_lo[1][:, h, 0:SEQ], M[3][:, 0:SEQ], f32(act_hi[1][:, h, 0:SEQ]), SUB).then_inc(sem["xo_lo"], 1)
                dve.wait_ge(sem["xo_lo"], now("xo_lo"))

            def da():
                dve.wait_ge(sem["pe_once"], before["xd_mm"] + 2)
                ts(dsc, G[0][:, 0:NMEM], cst[:, C_GS:C_GS + 1], MUL).then_inc(sem["dve_step"], 1)
                dve.wait_ge(sem["dve_step"], now())
                for b in range(1, DB):
                    stt(dsc, G[b // 2][:, (b % 2) * NMEM:(b % 2 + 1) * NMEM], cst[:, C_GS + b:C_GS + b + 1], dsc, MUL,
                        ADD).then_inc(sem["dve_step"], 1)
                    dve.wait_ge(sem["dve_step"], now())
                dve.memset(pdT[:, :, P:P + 16], 0.0).then_inc(sem["dve_step"], 1)
                dve.wait_ge(sem["dve_step"], now())
                dve.tensor_reduce(sm_(MX + 3), dsc, AX.X, MAX).then_inc(sem["dve_step"], 1)
                dve.wait_ge(sem["dve_step"], now())
                ts(sm_(NM + 3), sm_(MX + 3), -(XHD ** -0.5), MUL).then_inc(sem["dve_once"], 1)
                dve.wait_ge(sem["dve_once"], now("xd_max"))

            def de():
                dve.wait_ge(sem["act_once"], before["xd_exp"] + 1)
                recip(sm_(SM + 3)).then_inc(sem["dve_step"], 1)
                dve.wait_ge(sem["dve_step"], now())
                ts(dsc, dsc, sm_(SM + 3), MUL).then_inc(sem["dve_once"], 1)
                dve.wait_ge(sem["dve_once"], now("xd_prob"))

            def dz():
                dve.wait_ge(sem["pe_once"], before["xdv_mm"] + 2)
                dve.wait_ge(sem["xo_mm"], XH)
                copy(od[:, 1, :], G[1][:, :]).then_inc(sem["dve_once"], 1)
                dve.wait_ge(sem["dve_once"], now("od_dve"))
                for half in range(2):
                    dve.wait_ge(sem["xo_hi"], XH + half + 1)
                    tt(dz_dst(act_lo, half), dz_src(half), f32(dz_dst(act_hi, half)), SUB).then_inc(sem["xo_lo"], 1)
                    dve.wait_ge(sem["xo_lo"], now("xo_lo"))

            do_cross = dict(ss=ss, xm=xm, xo=xo, da=da, de=de, dz=dz)

            for n in range(8):
                split(4 * WQ + n + RING - 1)
                if n == 1:
                    dve.wait_ge(sem["rs_root"], 1)
                    recip(rstd[:, :]).then_inc(sem["rstd_new"], 1)
                    dve.wait_ge(sem["rstd_new"], now("rstd_new"))
                if n % 4 == 3:
                    for j in range(2):
                        h = 2 * (n // 4) + j
                        if j == 0:
                            dve.wait_ge(sem["tile0_done"], WQ + n // 4 + 1)
                        else:
                            dve.wait_ge(sem["chunk_used"], 4 * WQ + n + 1)
                        tt(qx[:, h, :], G[(TL_WQ + h) % GB][:, 0:NT], rstd[:, :], MUL).then_inc(sem["tile_out"], 1)
                        dve.wait_ge(sem["tile_out"], now("tile_out"))
                for what, h in beside_wq.get(n, ()):
                    ss(h)
            for what in cross:
                if what[0] in do_cross:
                    do_cross[what[0]](*what[1:])

            for n in range(8):
                split(CH_WO + n + RING - 1)
                for j in range(2):
                    if j == 0:
                        dve.wait_ge(sem["tile0_done"], WO + n + 1)
                    else:
                        dve.wait_ge(sem["chunk_used"], CH_WO + n + 1)
                    add_x(2 * n + j, TL_WO + 2 * n + j)
                for j in range(2):
                    m = 2 * n + j
                    dve.wait_ge(sem["ffn_hi"], m + 1)
                    stt(act_lo[0][:, m, :], xT[:, m, :], gcol[:, 48 + m:49 + m], f32(act_hi[0][:, m, :]), MUL,
                        SUB).then_inc(sem["ffn_lo"], 1)
                    dve.wait_ge(sem["ffn_lo"], now("ffn_lo"))
            def up(q, i, skip=0, first=False):
                for n in range(8):
                    split(CH_FFN + 8 * skip + n + RING - 1, q * 64 + i * 8)
                    if first and n == 1:
                        dve.wait_ge(sem["rs_root"], 2)
                        recip(rstd[:, :]).then_inc(sem["rstd_new"], 1)
                        dve.wait_ge(sem["rstd_new"], now("rstd_new"))
                    if n % 4 == 3:
                        g = n // 4
                        for j in range(2):
                            if j == 0:
                                dve.wait_ge(sem["tile0_done"], q * 16 + i * 2 + (FFN + 2 * skip + g + 1))
                            else:
                                dve.wait_ge(sem["chunk_used"], q * 64 + i * 8 + (CH_FFN + 8 * skip + n + 1))
                            stt(ur[:, j, :], G[(TL_FFN + 2 * g + j) % GB][:, 0:NT], 0.0, rstd[:, :], MAX,
                                MUL).then_inc(sem["tile_out"], 1)
                            dve.wait_ge(sem["tile_out"], now("tile_out"))
                            tt(us[:, j, :], ur[:, j, :], ur[:, j, :], MUL).then_inc(sem["dve_step"], 1)
                            dve.wait_ge(sem["dve_step"], now())
                        for j in range(2):
                            m = 2 * g + j
                            at = bass.ds(i * 4 + (4 * (skip % 4) + m), 1)
                            dve.wait_ge(sem["u_hi"], q * 16 + i * 4 + (16 * (skip // 8) + 4 * (skip % 4) + m + 1))
                            tt(act_lo[1][:, at, :].rearrange("p a b -> p (a b)"), us[:, j, :],
                               f32(act_hi[1][:, at, :]).rearrange("p a b -> p (a b)"), SUB).then_inc(sem["u_lo"], 1)
                            dve.wait_ge(sem["u_lo"], now("u_lo"))

            def down(q, i, skip=0, last=False, reg=True):
                for n in range(8):
                    if not last or n < RING + 1:
                        split(CH_FFN + 16 * skip + 32 + n + RING - 1, q * 64 + i * 8)
                    if n % 4 == 3:
                        g = n // 4
                        for j in range(2):
                            if j == 0:
                                dve.wait_ge(sem["tile0_done"], q * 16 + i * 2 + (FFN + 4 * skip + 8 + g + 1))
                            else:
                                dve.wait_ge(sem["chunk_used"], q * 64 + i * 8 + (CH_FFN + 16 * skip + 32 + n + 1))
                            if reg:
                                add_x(2 * g + j, TL_FFN + 2 * g + j, i)
                            else:
                                add_x(4 * i + 2 * g + j, TL_FFN + 2 * g + j)

            up(0, 0, first=True)
            with now.loop(3, tile_out=4, u_lo=4, own=4) as i:
                up(0, i, skip=1)
            with now.loop(4, tile_out=4) as i:
                down(0, i)
            with now.loop(2, tile_out=32, u_lo=16, own=16) as q:
                with now.loop(4, tile_out=4, u_lo=4, own=4) as i:
                    up(q, i, skip=8)
                with now.loop(4, tile_out=4) as i:
                    down(q, i, skip=4)
            with now.loop(4, tile_out=4, u_lo=4, own=4) as i:
                up(3, i)
            with now.loop(3, tile_out=4) as i:
                down(3, i)
            down(3, 3, last=True, reg=False)
            for o in range(0, 12, 2):
                dve.wait_ge(sem["y_T"], o + 1)
                copy(*y_piece(o)).then_inc(sem["y_dve"], 1)
                dve.wait_ge(sem["y_dve"], now("y_dve"))

        @block.gpsimd
        def _(pool):
            now = Counts(pool, "pool_step")

            def move(dst, src, signal):
                pool.dma_start(dst, src, allow_slow_non_contiguous=dst.ap[-1][1] == 1 or dst.ap[-1][0] != 1).then_inc(
                    signal, 16)

            pool.wait_ge(sem["dve_once"], before["relb_set"] + 1)
            move(relb[0:NB, :], ins["rel_bias"], sem["rel_in"])
            for what, to in (("cache_swa_k", "s_swa_k"), ("cache_swa_v", "s_swa_v")):
                move(outs[to][0, :, 0:WIN - DL, :, :].rearrange("b w k d -> b (w k d)"),
                     ins[what][0, :, DL:WIN, :, :].rearrange("b w k d -> b (w k d)"), sem["stored"])
            for k in range(4):
                pool.wait_ge(sem["x_stage"], 4 * k + 4)
                move(x_scr[:, 4 * k:4 * k + 4, :], xstage, sem["xscr_out"])
            pool.wait_ge(sem["x_T"], 16)
            move(scrow, ins["state_conv"].rearrange("o b w c -> (o b w) c"), sem["state_in"])
            move(n0row, ins["state_n"].rearrange("o b h d -> (o b h) d"), sem["state_in"])
            pool.wait_ge(sem["dve_once"], before["memk_ready"] + 8)
            pool.wait_ge(sem["tile_out"], 8)
            for kv, to in ((0, "p_mem_k"), (1, "p_mem_v")):
                move(outs[to].rearrange("o b (j p) h d -> p (o b j) (h d)", p=P), kvm[:, :, kv, :], sem["memkv_out"])
            pool.wait_ge(sem["act_once"], before["gate_rows"] + 1)
            move(outs["p_m"].rearrange("o b h -> h (o b)"), rows[:, 320 + SEQ - 1:320 + SEQ], sem["stored"])
            move(outs["s_m"].rearrange("o b h -> h (o b)"),
                 rows[:, 320 + SEQ:608].rearrange("p (b l) -> p b l", l=DL)[:, :, DL - 1], sem["stored"])
            pool.wait_ge(sem["dve_once"], before["bias_out"] + 5)
            move(b_scr, biasrow, sem["bscr_out"])
            pool.wait_ge(sem["bscr_out"], 16)
            pool.wait_ge(sem["memkv_out"], 32)
            pool.wait_ge(sem["xscr_out"], 64)

            def bias_load(t):
                if t >= 2:
                    pool.wait_ge(sem["sw_max"], t - 1)
                src = bass.AP(b_scr.tensor, 2 * t * NE, [[1, P], [NE, 2], [1, 256]])
                move(bias_t[:, t % 2], src, sem["bt_in"][t % 2])

            for what, to in (("cache_swa_k", kcache), ("cache_swa_v", vcache)):
                move(to, ins[what][0].rearrange("b w k d -> w b (k d)"), sem["swa_cache"])
            bias_load(0)
            bias_load(1)
            pool.wait_ge(sem["act_once"], before["ktok_out"] + 2)
            pool.wait_ge(sem["dve_once"], before["vtok_out"] + 2)
            for tok, p_to, s_to in ((ktok, "p_swa_k", "s_swa_k"), (vtok, "p_swa_v", "s_swa_v")):
                move(outs[p_to].rearrange("o b w k d -> (o b w) (k d)"), tok[:, 1, :], sem["swa_new_out"])
                for b in range(DB):
                    move(outs[s_to][0, b, WIN - DL:WIN].rearrange("l k d -> l (k d)"),
                         tok[DL * b:DL * b + DL, 2, :], sem["swa_new_out"])
            for t in range(2, 8):
                bias_load(t)

            def c_load(u):
                h, b0 = u // 2, 4 * (u % 2)
                move(cring[:, u % 3, :, 0:MDV], ins["state_C"][0, b0:b0 + 4, h].rearrange("b k v -> k b v"),
                     sem["c_in"][u % 3])

            pool.wait_ge(sem["av_mm"], 8)
            pool.wait_ge(sem["a_lo"], 8)
            pool.wait_ge(sem["swa_new_out"], 16 * 18)
            for u in range(3):
                c_load(u)

            def k_load(s, src):
                move(kraw[:, s], src, sem["kc_in"][s])

            def k_of(b):
                return ins["cache_mem_k"][0, b].rearrange("(j p) h d -> p j (h d)", p=P)

            pool.wait_ge(sem["v_out"], 16)
            pool.wait_ge(sem["conv_done"], 8)
            pool.wait_ge(sem["conv_sig"], 16)
            k_load(0, k_of(0))
            k_load(1, k_of(1))
            for h in range(MH):
                pool.wait_ge(sem["kwd_ready"], h + 1)
                pool.tensor_tensor(kwm, kwd.unsqueeze(1).to_broadcast([ND, DB, P]),
                                   sm_(WM + DB * h, DB, ND).unsqueeze(2).to_broadcast([ND, DB, P]),
                                   ALU.mult).then_inc(sem["kwm_ready"], 1)
                pool.wait_ge(sem["kwm_ready"], now("kwm_ready"))
                pool.wait_ge(sem["cp_out"], h + 1)
                move(outs["p_C"][0, 0, h], cprm[:, 0:MDV], sem["cp_dma"])
                for u in (2 * h, 2 * h + 1):
                    pool.wait_ge(sem["c_upd"], 4 * u + 4)
                    b0 = 4 * (u % 2)
                    move(outs["s_C"][0, b0:b0 + 4, h].rearrange("b k v -> k b v"), cring[:, u % 3, :, 0:MDV],
                         sem["c_out"][u % 3])
                    if u + 3 < 8:
                        pool.wait_ge(sem["n_col"], u + 1)
                        pool.wait_ge(sem["c_out"][u % 3], 16 * (u // 3 + 1))
                        c_load(u + 3)
            pool.wait_ge(sem["c_out"][0], 48)
            pool.wait_ge(sem["c_out"][1], 48)
            pool.wait_ge(sem["c_out"][2], 32)
            pool.wait_ge(sem["n_col"], 8)
            pool.wait_ge(sem["cp_dma"], 64)
            pool.wait_ge(sem["m_lo"], 8)
            pool.wait_ge(sem["m_hi"], 8)
            move(xT, x_scr, sem["xT_in"])
            move(vmem, outs["p_mem_v"].rearrange("o b (j p) h d -> p (o b j) (h d)", p=P), sem["vm_in"])

            def square(x, more=0, tile=0):
                pool.wait_ge(sem["tile_out"], more + (tile + 1))
                pool.tensor_tensor(nsq[:, :], x, x, ALU.mult).then_inc(sem["sq_step"], 1)
                pool.wait_ge(sem["sq_step"], now("sq_step"))
                pool.tensor_tensor(nacc[:, :], nacc[:, :], nsq[:, :], ALU.add).then_inc(sem["sq_sum"], 1)
                pool.wait_ge(sem["sq_sum"], now("sq_sum"))

            def x_tile(i, m):
                return xT[:, bass.ds(i * 4 + m, 1), :].rearrange("p a b -> p (a b)")

            pool.memset(nacc[:, :], 0.0).then_inc(sem["pool_step"], 1)
            pool.wait_ge(sem["pool_step"], now())
            with now.loop(3, sq_step=4, sq_sum=4) as i:
                for s in range(2):
                    src = ins["cache_mem_k"][0, bass.ds(pool.snap(i * 2 + (2 + s)), 1)].rearrange(
                        "b (j p) h d -> p (b j) (h d)", p=P)
                    pool.wait_ge(sem["kd_T"], i * 2 + (s + 1))
                    k_load(s, src)
                    for m in (2 * s, 2 * s + 1):
                        square(x_tile(i, m), i * 4, TL_WOUT + m)
            for s in range(2):
                if s == 0:
                    pool.wait_ge(sem["kd_T"], 7)
                    move(kraw[:, 0], outs["p_mem_k"].rearrange("o b (j p) h d -> p (o b j) (h d)", p=P), sem["km_in"])
                for m in (2 * s, 2 * s + 1):
                    square(xT[:, 12 + m, :], 0, TL_WOUT + 12 + m)
            pool.wait_ge(sem["act_once"], before["tail_out"] + 2)
            pool.wait_ge(sem["act_once"], before["ncol_out"] + 1)
            move(outs["p_conv"].rearrange("o b w c -> (o b w) c"), stail_late[0:3, :], sem["tail_dma"])
            move(outs["s_conv"].rearrange("o b w c -> (o b w) c"), stail_late[3:27, :], sem["tail_dma"])
            move(outs["p_n"].rearrange("o b h d -> (o b h) d"), nrow[0:4, :], sem["tail_dma"])
            move(outs["s_n"].rearrange("o b h d -> (o b h) d"), nrow[4:36, :], sem["tail_dma"])
            for b in range(DB):
                if b % 4 == 0:
                    pool.wait_ge(sem["pe_once"], before["xd_mm"] + b // 4 + 1)
                move(vdec[:, b], ins["cache_mem_v"][0, b].rearrange("(j p) h d -> p j (h d)", p=P),
                     sem["vdec_in"][b // 4])
            pool.wait_ge(sem["ss_all"], 1)
            pool.memset(nacc[:, :], 0.0).then_inc(sem["pool_step"], 1)
            pool.wait_ge(sem["pool_step"], now())
            for m in range(KT):
                square(xT[:, m, :], 0, TL_WO + m)
            for o in range(12):
                kt4, j = divmod(o, 3)
                n = P if j < 2 else ND
                if o % 2:
                    pool.wait_ge(sem["y_act"], o // 2 + 1)
                else:
                    pool.wait_ge(sem["y_dve"], o // 2 + 1)
                dst = (outs["y_prompt"][0, j * P:(j + 1) * P, :] if j < 2
                       else outs["y_sample"].rearrange("b l d -> (b l) d"))
                move(dst[:, kt4 * 512:(kt4 + 1) * 512], ytok[0:n, j, kt4 * 512:(kt4 + 1) * 512], sem["stored"])
            pool.wait_ge(sem["stored"], 16 * 16)
            pool.wait_ge(sem["tail_dma"], 64)
            pool.wait_ge(sem["cp_dma"], 64)
            pool.wait_ge(sem["c_out"][0], 48)
            pool.wait_ge(sem["c_out"][1], 48)
            pool.wait_ge(sem["c_out"][2], 32)
            pool.wait_ge(sem["swa_new_out"], 16 * 18)
            pool.wait_ge(sem["memkv_out"], 32)


_INS = ['x_prompt', 'x_sample', 'mem_prompt', 'state_conv', 'state_C', 'state_n', 'state_m', 'cache_swa_k',
        'cache_swa_v', 'cache_mem_k', 'cache_mem_v', 'norm_mix', 'w_in', 'conv_w', 'conv_b', 'b_igate', 'b_fgate',
        'm_out_norm', 'q_norm_a', 'k_norm_a', 'sinks', 'w_out', 'rel_bias', 'norm_x', 'norm_mem', 'wq_x', 'wk_x',
        'wv_x', 'q_norm_x', 'k_norm_x', 'wo_x', 'norm_ffn', 'w_up', 'w_down']
_OUTS = [('y_prompt', (1, SEQ, D)), ('y_sample', (DB, DL, D)),
         ('p_conv', (1, 1, 3, CONVC)), ('p_C', (1, 1, MH, MDK, MDV)), ('p_n', (1, 1, MH, MDK)), ('p_m', (1, 1, MH)),
         ('p_swa_k', (1, 1, WIN, KVH, HD)), ('p_swa_v', (1, 1, WIN, KVH, HD)),
         ('p_mem_k', (1, 1, NMEM, XH, XHD)), ('p_mem_v', (1, 1, NMEM, XH, XHD)),
         ('s_conv', (1, DB, 3, CONVC)), ('s_C', (1, DB, MH, MDK, MDV)), ('s_n', (1, DB, MH, MDK)),
         ('s_m', (1, DB, MH)), ('s_swa_k', (1, DB, WIN, KVH, HD)), ('s_swa_v', (1, DB, WIN, KVH, HD))]


def kernel(**inputs):
    import concourse.bacc as bacc
    from concourse.bass_utils import run_bass_kernel_spmd

    nc = bacc.Bacc("TRN2", target_bir_lowering=False, num_devices=1)
    arrays, ins, outs = {}, {}, {}
    for name in _INS:
        a = np.ascontiguousarray(inputs[name])
        arrays[f"in_{name}"] = a
        ins[name] = nc.dram_tensor(f"in_{name}", a.shape, mybir.dt.from_np(a.dtype), kind="ExternalInput").ap()
    c = constants()
    arrays["in_consts"] = c
    consts = nc.dram_tensor("in_consts", c.shape, F32, kind="ExternalInput").ap()
    for name, shape in _OUTS:
        outs[name] = nc.dram_tensor(f"out_{name}", shape, F32, kind="ExternalOutput").ap()
    layer_kernel(nc, ins, outs, consts)
    r = run_bass_kernel_spmd(nc, [arrays], core_ids=[0])
    return tuple(r.results[0][f"out_{name}"] for name, _ in _OUTS)
```
